# Optimizing a Trainium2 kernel written in Bass

```python
import math
import jax, jax.numpy as jnp
from jax import lax
import numpy as np

D_MODEL = 1024
BATCH = 1
SEQ = 1024
DEPTH = 1

CHUNK = 64
N_MEM = 256
N_GROUPS = 4
GROUP = D_MODEL // N_GROUPS
D_MIX = N_GROUPS * GROUP
N_HEADS = 4
HEAD_DIM = GROUP // N_HEADS
RWKV_LORA = 32
CONV_WIDTH = 31
SB_BLOCK = 128
XATTN_HEADS = 4
XATTN_HEAD_DIM = D_MODEL // XATTN_HEADS
RMS_EPS = 1e-6
LN_EPS = 1e-5
RWKV_LN_EPS = 64e-5

N_RWKV_SHIFT = 3 * GROUP + 2 * RWKV_LORA
N_RWKV = N_RWKV_SHIFT + GROUP
N_CONV = 3 * GROUP
N_HGRN = 4 * GROUP
N_SB = 4 * GROUP
N_IN = N_RWKV + N_CONV + N_HGRN + N_SB

kernel_name = 'hybrid_parallel_heads_rwkv7_conformer_hgrn2_stickbreak'

def rms_norm(x, g):
    x32 = x.astype(jnp.float32)
    y = x32 * lax.rsqrt(jnp.mean(x32 * x32, axis=-1, keepdims=True) + RMS_EPS)
    return (y * g.astype(jnp.float32)).astype(x.dtype)

def layer_norm_f32(x, g, b, eps):
    x32 = x.astype(jnp.float32)
    mu = jnp.mean(x32, axis=-1, keepdims=True)
    xc = x32 - mu
    var = jnp.mean(xc * xc, axis=-1, keepdims=True)
    return xc * lax.rsqrt(var + eps) * g + b

def split_heads(t):
    return t.reshape(*t.shape[:-1], N_HEADS, HEAD_DIM)

def rwkv7_mixer(p_shift, gate, mu, w0, w_up, a0, a_up, k_k, k_a, r_k, ln_g, ln_b):
    B, T, _ = p_shift.shape
    p = p_shift.astype(jnp.float32)
    p_prev = jnp.pad(p, ((0, 0), (1, 0), (0, 0)))[:, :-1]
    m = p + (p_prev - p) * mu
    r, k, v, xw, xa = jnp.split(m, [GROUP, 2 * GROUP, 3 * GROUP, 3 * GROUP + RWKV_LORA], axis=-1)
    w_log = -jax.nn.softplus(-(w0 + jnp.tanh(xw) @ w_up)) - 0.5
    decay = jnp.exp(-jnp.exp(w_log))
    a = jax.nn.sigmoid(a0 + xa @ a_up)
    kk = split_heads(k * k_k)
    kk = kk / jnp.maximum(jnp.sqrt(jnp.sum(kk * kk, axis=-1, keepdims=True)), 1e-12)
    k = k * (1.0 + (a - 1.0) * k_a)
    r, k, v, decay, a = (split_heads(t) for t in (r, k, v, decay, a))
    xs = tuple(jnp.moveaxis(t, 1, 0) for t in (r, decay, k, v, -kk, kk * a))

    def step(S, inp):
        r_t, w_t, k_t, v_t, a_t, b_t = inp
        sa = jnp.einsum('bhij,bhj->bhi', S, a_t)
        S = S * w_t[:, :, None, :] + sa[..., None] * b_t[:, :, None, :] + v_t[..., None] * k_t[:, :, None, :]
        y = jnp.einsum('bhij,bhj->bhi', S, r_t)
        return S, y

    S0 = jnp.zeros((B, N_HEADS, HEAD_DIM, HEAD_DIM), jnp.float32)
    _, y = lax.scan(step, S0, xs)
    y = jnp.moveaxis(y, 0, 1)
    y = layer_norm_f32(y, ln_g.reshape(N_HEADS, HEAD_DIM), ln_b.reshape(N_HEADS, HEAD_DIM), RWKV_LN_EPS)
    bonus = jnp.sum(r * k * r_k, axis=-1, keepdims=True) * v
    out = (y + bonus).reshape(B, T, GROUP)
    return out * jax.nn.silu(gate.astype(jnp.float32))

def conformer_conv_mixer(val, glu_gate, gate, conv_w, conv_b, ln_g, ln_b):
    u = val * jax.nn.sigmoid(glu_gate)
    u = jnp.pad(u, ((0, 0), (CONV_WIDTH - 1, 0), (0, 0)))
    y = lax.conv_general_dilated(u, conv_w[:, None, :].astype(u.dtype), window_strides=(1,), padding='VALID',
                                 dimension_numbers=('NWC', 'WIO', 'NWC'), feature_group_count=GROUP)
    y = layer_norm_f32(y + conv_b, ln_g, ln_b, LN_EPS)
    y = jax.nn.silu(y)
    return y * jax.nn.silu(gate.astype(jnp.float32))

def hgrn2_mixer(q, f_pre, i, gate, lb, norm_g):
    B, T, _ = q.shape
    n_chunks = T // CHUNK
    q = jax.nn.silu(q.astype(jnp.float32))
    f = lb + (1.0 - lb) * jax.nn.sigmoid(f_pre.astype(jnp.float32))
    log_f = jnp.log(f)
    k = 1.0 - f
    v = i.astype(jnp.float32)

    def to_chunks(t):
        return t.reshape(B, n_chunks, CHUNK, N_HEADS, HEAD_DIM).transpose(1, 0, 3, 2, 4)

    qc, kc, vc = to_chunks(q), to_chunks(k), to_chunks(v)
    bc = jnp.cumsum(to_chunks(log_f), axis=3)
    causal = (jnp.arange(CHUNK)[:, None] >= jnp.arange(CHUNK)[None, :])[:, :, None]

    def chunk_step(S, inp):
        q_c, k_c, v_c, b_c = inp
        o_inter = jnp.einsum('bhtk,bhkv->bhtv', q_c * jnp.exp(b_c), S)
        rel = jnp.where(causal, b_c[:, :, :, None, :] - b_c[:, :, None, :, :], -jnp.inf)
        att = jnp.einsum('bhtk,bhsk,bhtsk->bhts', q_c, k_c, jnp.exp(rel))
        o_intra = jnp.einsum('bhts,bhsv->bhtv', att, v_c)
        b_last = b_c[:, :, -1:, :]
        S = jnp.exp(b_last[:, :, 0, :])[..., None] * S + jnp.einsum('bhsk,bhsv->bhkv', k_c * jnp.exp(b_last - b_c), v_c)
        return S, o_inter + o_intra

    S0 = jnp.zeros((B, N_HEADS, HEAD_DIM, HEAD_DIM), jnp.float32)
    _, o = lax.scan(chunk_step, S0, (qc, kc, vc, bc))
    o = o.transpose(1, 0, 3, 2, 4).reshape(B, T, N_HEADS, HEAD_DIM)
    o = o * lax.rsqrt(jnp.mean(o * o, axis=-1, keepdims=True) + RMS_EPS) * norm_g.reshape(N_HEADS, HEAD_DIM)
    return o.reshape(B, T, GROUP) * jax.nn.silu(gate.astype(jnp.float32))

def stick_breaking_mixer(q, k, v, gate):
    B, T, _ = q.shape

    def heads(t):
        return t.astype(jnp.float32).reshape(B, T, N_HEADS, HEAD_DIM).transpose(0, 2, 1, 3)

    qh, kh, vh = heads(q), heads(k), heads(v)
    scale = HEAD_DIM ** -0.5
    outs = []
    for blk in range(T // SB_BLOCK):
        lo, hi = blk * SB_BLOCK, (blk + 1) * SB_BLOCK
        z = jnp.einsum('bhtd,bhsd->bhts', qh[:, :, lo:hi], kh[:, :, :hi]) * scale
        t_idx = lo + jnp.arange(SB_BLOCK)
        mask = jnp.arange(hi)[None, :] < t_idx[:, None]
        log_keep = jnp.where(mask, jax.nn.log_sigmoid(-z), 0.0)
        tail = lax.cumsum(log_keep, axis=3, reverse=True) - log_keep
        A = jnp.where(mask, jnp.exp(jax.nn.log_sigmoid(z) + tail), 0.0)
        outs.append(jnp.einsum('bhts,bhsd->bhtd', A, vh[:, :, :hi]))
    o = jnp.concatenate(outs, axis=2).transpose(0, 2, 1, 3).reshape(B, T, GROUP)
    return o * jax.nn.silu(gate.astype(jnp.float32))

def memory_cross_attention(h, mem_n, wq, wk, wv, wo):
    B, T, _ = h.shape
    M = mem_n.shape[1]
    q = (h @ wq).reshape(B, T, XATTN_HEADS, XATTN_HEAD_DIM)
    k = (mem_n @ wk).reshape(B, M, XATTN_HEADS, XATTN_HEAD_DIM)
    v = (mem_n @ wv).reshape(B, M, XATTN_HEADS, XATTN_HEAD_DIM)
    s = jnp.einsum('bthd,bmhd->bhtm', q, k).astype(jnp.float32) * (XATTN_HEAD_DIM ** -0.5)
    p = jax.nn.softmax(s, axis=-1).astype(h.dtype)
    o = jnp.einsum('bhtm,bmhd->bthd', p, v).reshape(B, T, D_MODEL)
    return o @ wo

def setup_inputs(seed: int = 0) -> dict:
    key = jax.random.key(seed)
    ks = jax.random.split(key, 32)
    f32 = jnp.float32
    nrm = lambda k, shape, s: jax.random.normal(k, shape, f32) * s
    gain = lambda k, shape: 1.0 + 0.02 * jax.random.normal(k, shape, f32)
    L = DEPTH
    return {
        'x': jax.random.normal(ks[0], (BATCH, SEQ, D_MODEL), f32),
        'mem': jax.random.normal(ks[1], (BATCH, N_MEM, D_MODEL), f32),
        'norm_mix': gain(ks[2], (L, D_MODEL)),
        'w_in': nrm(ks[3], (L, D_MODEL, N_IN), D_MODEL ** -0.5),
        'rwkv_mu': jax.random.uniform(ks[4], (L, N_RWKV_SHIFT), f32),
        'rwkv_w0': jax.random.uniform(ks[5], (L, GROUP), f32, minval=-6.0, maxval=1.0),
        'rwkv_w_up': nrm(ks[6], (L, RWKV_LORA, GROUP), 0.1),
        'rwkv_a0': nrm(ks[7], (L, GROUP), 0.1),
        'rwkv_a_up': nrm(ks[8], (L, RWKV_LORA, GROUP), 0.1),
        'rwkv_k_k': 0.85 + 0.05 * jax.random.normal(ks[9], (L, GROUP), f32),
        'rwkv_k_a': gain(ks[10], (L, GROUP)),
        'rwkv_r_k': nrm(ks[11], (L, N_HEADS, HEAD_DIM), 0.1),
        'rwkv_ln_g': gain(ks[12], (L, GROUP)),
        'rwkv_ln_b': nrm(ks[13], (L, GROUP), 0.02),
        'conv_w': nrm(ks[14], (L, CONV_WIDTH, GROUP), CONV_WIDTH ** -0.5),
        'conv_b': nrm(ks[15], (L, GROUP), 0.02),
        'conv_ln_g': gain(ks[16], (L, GROUP)),
        'conv_ln_b': nrm(ks[17], (L, GROUP), 0.02),
        'hgrn_lb_logits': nrm(ks[18], (L, GROUP), 0.5),
        'hgrn_norm_g': gain(ks[19], (L, GROUP)),
        'w_out': nrm(ks[20], (L, D_MIX, D_MODEL), D_MIX ** -0.5),
        'norm_xattn': gain(ks[21], (L, D_MODEL)),
        'norm_mem': gain(ks[22], (L, D_MODEL)),
        'xattn_wq': nrm(ks[23], (L, D_MODEL, D_MODEL), D_MODEL ** -0.5),
        'xattn_wk': nrm(ks[24], (L, D_MODEL, D_MODEL), D_MODEL ** -0.5),
        'xattn_wv': nrm(ks[25], (L, D_MODEL, D_MODEL), D_MODEL ** -0.5),
        'xattn_wo': nrm(ks[26], (L, D_MODEL, D_MODEL), D_MODEL ** -0.5),
        'norm_final': gain(ks[27], (D_MODEL,)),
    }

def reference(x, mem, norm_mix, w_in, rwkv_mu, rwkv_w0, rwkv_w_up, rwkv_a0, rwkv_a_up, rwkv_k_k, rwkv_k_a,
              rwkv_r_k, rwkv_ln_g, rwkv_ln_b, conv_w, conv_b, conv_ln_g, conv_ln_b, hgrn_lb_logits, hgrn_norm_g,
              w_out, norm_xattn, norm_mem, xattn_wq, xattn_wk, xattn_wv, xattn_wo, norm_final):
    lb_soft = jax.nn.softmax(hgrn_lb_logits.astype(jnp.float32), axis=0)
    lower_bounds = jnp.cumsum(lb_soft, axis=0) - lb_soft[0]
    splits = [N_RWKV, N_RWKV + N_CONV, N_RWKV + N_CONV + N_HGRN]
    for l in range(DEPTH):
        h = rms_norm(x, norm_mix[l])
        p = h @ w_in[l]
        p_a, p_b, p_c, p_d = jnp.split(p, splits, axis=-1)
        y_a = rwkv7_mixer(p_a[..., :N_RWKV_SHIFT], p_a[..., N_RWKV_SHIFT:], rwkv_mu[l], rwkv_w0[l], rwkv_w_up[l],
                          rwkv_a0[l], rwkv_a_up[l], rwkv_k_k[l], rwkv_k_a[l], rwkv_r_k[l], rwkv_ln_g[l], rwkv_ln_b[l])
        c_val, c_glu, c_gate = jnp.split(p_b, 3, axis=-1)
        y_b = conformer_conv_mixer(c_val, c_glu, c_gate, conv_w[l], conv_b[l], conv_ln_g[l], conv_ln_b[l])
        g_q, g_f, g_i, g_gate = jnp.split(p_c, 4, axis=-1)
        y_c = hgrn2_mixer(g_q, g_f, g_i, g_gate, lower_bounds[l], hgrn_norm_g[l])
        s_q, s_k, s_v, s_gate = jnp.split(p_d, 4, axis=-1)
        y_d = stick_breaking_mixer(s_q, s_k, s_v, s_gate)
        y = jnp.concatenate([y_a, y_b, y_c, y_d], axis=-1).astype(x.dtype)
        x = x + y @ w_out[l]
        hx = rms_norm(x, norm_xattn[l])
        mn = rms_norm(mem, norm_mem[l])
        x = x + memory_cross_attention(hx, mn, xattn_wq[l], xattn_wk[l], xattn_wv[l], xattn_wo[l])
    return rms_norm(x, norm_final)


_drawn_inputs = setup_inputs


def setup_inputs(seed=0):
    import zlib

    import numpy as np

    out = dict(_drawn_inputs(seed))
    spreads = {}
    factors = {'norm_mix': 3.543,
     'rwkv_w_up': 7.554,
     'rwkv_a0': 5.24,
     'rwkv_k_k': 34.296,
     'rwkv_k_a': 8.0,
     'rwkv_ln_g': 64.0,
     'rwkv_ln_b': 64.0,
     'conv_b': 33.845,
     'conv_ln_g': 64.0,
     'conv_ln_b': 64.0,
     'hgrn_norm_g': 64.0,
     'norm_xattn': 24.647,
     'norm_mem': 28.093,
     'norm_final': 9.758}
    for name, (base, spread) in spreads.items():
        noise = np.random.default_rng([zlib.crc32(name.encode()), seed]).standard_normal(out[name].shape)
        drawn = base * np.exp(spread * noise) if base else spread * noise
        out[name] = __import__('jax').numpy.asarray(drawn.astype(out[name].dtype))
    for name, factor in factors.items():
        out[name] = (out[name] * factor).astype(out[name].dtype)
    return out
```

```python
from contextlib import ExitStack

import numpy as np

import concourse.bass as bass
from concourse import mybir

F32 = mybir.dt.float32
F32R = mybir.dt.float32r
U8 = mybir.dt.uint8
ALU = mybir.AluOpType
ACT = mybir.ActivationFunctionType
AX = mybir.AxisListType

P = 128
D = 1024
T = 1024
M = 256
KT = D // P
TT = T // P
G = 256
CH = 64
NC = T // CH
HD = 64
CW = 31
HALF = 512
RMS_EPS, LN_EPS, RWKV_EPS = 1e-6, 1e-5, 64e-5
DECAY = -float(np.exp(-0.5))
LN_FLOOR = 2.0 ** -63
KK_SCALE = 2.0 ** 16

C_R, C_K, C_V, C_XW, C_RG = 0, 256, 512, 768, 832
C_CV, C_CG, C_CGATE = 1088, 1344, 1600
C_HQ, C_HF, C_HI, C_HG = 1856, 2112, 2368, 2624
C_SQ, C_SK, C_SV, C_SG = 2880, 3136, 3392, 3648

CHAN = {}
_at = 0
for _n, _k in (("mu", 6), ("mux", 1), ("w0", 2), ("a0", 2), ("k_k", 2), ("k_a", 2), ("r_k", 2), ("rln_g", 2),
               ("rln_b", 2), ("cw", 2 * CW), ("cb", 2), ("cln_g", 2), ("cln_b", 2), ("hn_g", 2), ("lbl", 2)):
    CHAN[_n] = _at
    _at += _k
N_CHAN = _at
DER = {"omu": 0, "omux": 6, "oka": 7, "e": 9, "soft": 11, "lb": 13, "omlb": 15, "eps": 17}
N_DER = 24
NORM_MIX, NORM_X, NORM_MEM, NORM_FIN = range(4)
EPS = (RMS_EPS, LN_EPS, RWKV_EPS)
N_CONSTS = 5
EXP_SET = "natural_log_exp_and_others"
SIG_SET = "sigmoid_and_others"


def sb_blocks(th):
    return list(range(4 * th + 3, -1, -1))


def sb_cols(th, j):
    a = max(j * P - th * HALF, 0)
    return a, HALF - a


def weight_columns(kind):
    g = kind[0]
    if g in ("mk", "mv", "q"):
        return {"mk": "wk", "mv": "wv", "q": "wq"}[g], kind[1] * P
    if g == "xw":
        return "w_in", C_XW
    first = {("rw", "r"): C_R, ("rw", "k"): C_K, ("rw", "v"): C_V, ("rw", "gate"): C_RG,
             ("cv", "val"): C_CV, ("cv", "glu"): C_CG, ("cv", "gate"): C_CGATE,
             ("h", "q"): C_HQ, ("h", "f"): C_HF, ("h", "i"): C_HI, ("h", "gate"): C_HG,
             ("s", "q"): C_SQ, ("s", "k"): C_SK, ("s", "v"): C_SV, ("s", "gate"): C_SG}[g, kind[2]]
    return "w_in", first + kind[1] * P


def schedule():
    s = [("xn", 0)]
    for i in range(TT):
        if i + 1 < TT:
            s.append(("xn", i + 1))
        s.append(("xT", i))
    p = lambda *k: s.append(("proj",) + k)
    p("xw")
    s.append(("xwt",))
    for i in range(2):
        p("cv", i, "glu")
        p("cv", i, "val")
    for i in range(2):
        for part in range(4):
            s.append(("conv", i, part))
    p("cv", 0, "gate")
    p("cv", 1, "gate")
    s += [("cmean",), ("csq",), ("cvar",), ("cfin",)]
    for i in range(2):
        s.append(("lora", i))
        for w in ("k", "r", "v"):
            p("rw", i, w)
        s += [("rwa", i), ("kkn", i), ("rwb", i), ("tok", "v", i), ("bon", i), ("tok", "b", i), ("tok", "k", i),
              ("minit", i)]
        p("rw", i, "gate")
        s += [("inv", i, l) for l in range(1, 6)]
        s += [("mk3", i)] + [("chunk", i, c) for c in range(NC)] + [("mu", i), ("var", i), ("rfin", i)]
    for i in range(2):
        for w in ("q", "k", "v", "gate"):
            p("s", i, w)
        s.append(("sv", i))
        s += [("sb", i, hd, th) for hd in range(2) for th in range(2)]
    for i in range(2):
        for w in ("f", "q", "i", "gate"):
            p("h", i, w)
        s += [("hgate", i), ("tok", "hv", i), ("hdiag", i)] + [("hlev", i, l) for l in range(6)]
        s += [("hbars", i), ("tok", "hk", i), ("hkv", i), ("hout", i), ("hvar", i), ("hfin", i)]
    s += [("mn", 0), ("mn", 1), ("mT", 0), ("mT", 1)]
    for n in range(KT):
        p("mk", n)
    for n in range(KT):
        p("mv", n)
        if n:
            s.append(("vtr", n - 1))
    s.append(("vtr", KT - 1))
    s += [("ysplit", i) for i in range(TT)]
    s += [("wide", "o", n, i) for n in range(3) for i in range(TT)]
    for i in range(TT + 1):
        if i < TT:
            s += [("wide", "o", 3, i), ("x2n", i)]
        if i:
            s.append(("hT", i - 1))
    for n in range(KT):
        p("q", n)
    at = [(i, g) for i in range(TT) for g in range(2)]
    for n in range(len(at) + 2):
        if n < len(at):
            s.append(("ascore",) + at[n])
        if 0 < n <= len(at):
            s.append(("aturn",) + at[n - 1])
        if n > 1:
            s.append(("aval",) + at[n - 2])
    s += [("wide", "f", n, i) for n in range(3) for i in range(TT)]
    for i in range(TT):
        s += [("wide", "f", 3, i), ("fin", i)]
    return s



def shape_constants():
    p = np.arange(P)
    f = np.zeros((P, 4 * P + 2 * CH), np.float32)
    f[:, 0:P] = np.eye(P)
    f[:, P:2 * P] = (p[:, None] // HD == p[None, :] // HD)
    f[:, 2 * P:3 * P] = -(p[:, None] >= p[None, :]).astype(np.float32)
    f[:, 3 * P:4 * P] = -1.0
    s, t = (p % CH)[:, None], np.arange(CH)[None, :]
    f[:, 4 * P:4 * P + CH] = s < t
    f[:, 4 * P + CH:] = s <= t
    m = np.zeros((P, 13 * CH), np.float32)
    for l in range(6):
        same = (s >> (l + 1)) == (t >> (l + 1))
        m[:, l * CH:(l + 1) * CH] = same & (((s >> l) & 1) == 0) & (((t >> l) & 1) == 1)
        m[:, (6 + l) * CH:(7 + l) * CH] = same & (((s >> l) & 1) == 1) & (((t >> l) & 1) == 0)
    m[:, 12 * CH:] = s == t
    return f, m


def program(nc, x, mem, w_in, w_out, wq, wk, wv, wo, lora, chan, norms, fconst, mconst, out):
    with ExitStack() as ctx:
        def sb(name, shape, dt=F32):
            return ctx.enter_context(nc.sbuf_tensor(name, shape, dt))

        act_hi = sb("act_hi", [P, KT, T], F32R)
        act_lo = sb("act_lo", [P, KT, T], F32R)
        yT = sb("yT", [P, KT, T])
        fcst = sb("fcst", [P, 4 * P + 2 * CH])
        mcst = sb("mcst", [P, 13 * CH], U8)
        chn = sb("chn", [P, N_CHAN])
        der = sb("der", [P, N_DER])
        lora_sb = sb("lora_sb", [64, G])
        reset = sb("reset", [P, T], U8)
        stat = sb("stat", [P, 96])
        S_st = sb("S_st", [P, 2, CH])
        R_sb = sb("R_sb", [P, CH])
        U_sb = sb("U_sb", [P, CH])
        DC = sb("DC", [P, NC])
        ident = fcst[:, 0:P]
        blk = fcst[:, P:2 * P]
        tri = fcst[:, 2 * P:3 * P]
        negone = fcst[:, 3 * P:4 * P]
        m_strict = fcst[:, 4 * P:4 * P + CH]
        m_incl = fcst[:, 4 * P + CH:4 * P + 2 * CH]

        def lev(l):
            return mcst[:, l * CH:(l + 1) * CH]

        with ExitStack() as st:
            wraw = st.enter_context(nc.sbuf_tensor("wraw", [P, 2, 4, P], F32))
            whi = st.enter_context(nc.sbuf_tensor("whi", [P, 2, KT, P], F32R))
            wlo = st.enter_context(nc.sbuf_tensor("wlo", [P, 2, KT, P], F32R))
        xa_scr = sb("xa_scr", [P, 5 * T])
        with ExitStack() as st:
            A = st.enter_context(nc.sbuf_tensor("A", [P, 12, T], F32))
            raw = st.enter_context(nc.sbuf_tensor("raw", [P, 1 + T], F32))
            xm = st.enter_context(nc.sbuf_tensor("xm", [64, T], F32))
            B = st.enter_context(nc.sbuf_tensor("B", [P, 7, T], F32))
        with ExitStack() as st:
            x2 = st.enter_context(nc.sbuf_tensor("x2", [P, TT, D], F32))
            vhi = st.enter_context(nc.sbuf_tensor("vhi", [P, 2, KT, 256], F32R))
            vlo0 = st.enter_context(nc.sbuf_tensor("vlo0", [P, KT, 256], F32R))
            _gap = st.enter_context(nc.sbuf_tensor("gap", [P, 1], F32))
            kv = st.enter_context(nc.sbuf_tensor("kv", [P, 4, T], F32))
            vlo1 = st.enter_context(nc.sbuf_tensor("vlo1", [P, KT, 256], F32R))
            vraw = st.enter_context(nc.sbuf_tensor("vraw", [P, 2, 2, 256], F32))

        banks = [ctx.enter_context(nc.psum_tensor(f"bank{i}", [P, HALF], F32)) for i in range(8)]

        sems, counts = {}, {}

        def sem(name):
            if name not in sems:
                sems[name] = ctx.enter_context(nc.semaphore(name))
            return sems[name]

        def done(eng, ins, name):
            counts[name] = counts.get(name, 0) + 1
            ins.then_inc(sem(name), 1)
            eng.wait_ge(sem(name), counts[name])

        class Ring:

            def __init__(self, name, ids):
                self.name, self.ids, self.units, self.n = name, ids, {}, 0
                self.posted, self.read = [0] * len(ids), [0] * len(ids)

            def plan(self, key, reads=1, posts=1):
                b = self.n % len(self.ids)
                self.units[key] = (b, self.posted[b], self.read[b], reads)
                self.n += 1
                self.posted[b] += posts
                self.read[b] += reads

            def bank(self, key):
                return banks[self.ids[self.units[key][0]]][:, :]

            def ready(self, b):
                return sem(f"{self.name}{b}_ready")

            def free(self, b):
                return sem(f"{self.name}{b}_free")

            def pe_open(self, pe, key):
                b, _, r, _ = self.units[key]
                if r:
                    pe.wait_ge(self.free(b), r)
                return self.bank(key)

            def pe_post(self, ins, key):
                ins.then_inc(self.ready(self.units[key][0]), 1)

            def rd_open(self, eng, key, post=1):
                b, n, _, _ = self.units[key]
                eng.wait_ge(self.ready(b), n + post)
                return self.bank(key)

            def rd_done(self, eng, ins, key, nth=1):
                b, _, r, _ = self.units[key]
                ins.then_inc(self.free(b), 1)
                eng.wait_ge(self.free(b), r + nth)

            def wait_read(self, eng, key, nth=None):
                b, _, r, k = self.units[key]
                eng.wait_ge(self.free(b), r + (k if nth is None else nth))

        pj = Ring("pj", [0, 1, 2])
        rw = Ring("rw", [3, 4])
        sz = Ring("sz", [5, 6])
        so = Ring("so", [7])
        av_ring = so

        SCHED = schedule()
        wsrc = {"w_in": w_in, "wk": wk, "wv": wv, "wq": wq}
        tiles = [a for name, *a in SCHED if name == "proj"]
        tile_no = {tuple(t): n for n, t in enumerate(tiles)}
        shifted = [t for t in tiles if t[0] == "xw" or (t[0] == "rw" and t[2] in "rkv")]
        shift_no = {tuple(t): n for n, t in enumerate(shifted)}
        for name, *a in SCHED:
            a = tuple(a)
            if name in ("xT", "mT", "hT"):
                for q in range(2):
                    pj.plan((name,) + a + (q,), reads=2)
            elif name == "proj":
                for h in range(1 if a[0] in ("mk", "mv") else 2):
                    pj.plan(a + (h,), reads=2 if a[-1] == "gate" or (a[0], a[-1]) == ("h", "q") else 1)
            elif name == "lora":
                for w in "za":
                    for h in range(2):
                        rw.plan((w,) + a + (h,))
            elif name in ("kkn", "bon", "mu", "var", "hvar", "hdiag", "hkv", "hout", "tok"):
                for h in range(2):
                    rw.plan((name,) + a + (h,))
            elif name == "minit":
                for h in range(2):
                    rw.plan(("L",) + a + (h,), reads=2)
                    rw.plan(("M",) + a + (h,))
            elif name == "inv":
                for w in ("P1", "dTT", "dT")[:3 if a[1] < 5 else 2]:
                    for h in range(2):
                        rw.plan((w,) + a + (h,))
            elif name == "mk3":
                for w in ("ak", "rb", "rk"):
                    for h in range(2):
                        rw.plan((w,) + a + (h,))
            elif name == "chunk":
                for w in ("R", "U", "S", "Y")[:4] if a[1] < NC - 1 else ("R", "U", "Y"):
                    rw.plan((w,) + a)
            elif name == "hlev":
                for h in range(2):
                    rw.plan(("hl",) + a + (h,))
            elif name in ("cmean", "cvar"):
                for h in range(2):
                    rw.plan((name, h), reads=2 if name == "cmean" else 1)
            elif name == "sv":
                for h in range(2):
                    sz.plan((name,) + a + (h,))
            elif name == "sb":
                p, hd, th = a
                for j in sb_blocks(th):
                    sz.plan(("z", p, hd, th, j), reads=2 if j >= 4 * th and sb_cols(th, j)[1] > P else 1, posts=2)
                so.plan(("o", p, hd, th))
            elif name in ("vtr", "wide"):
                pj.plan((name,) + a)
            elif name == "ascore":
                rw.plan((name,) + a, reads=2)
            elif name == "aturn":
                sz.plan((name,) + a)
            elif name == "aval":
                av_ring.plan((name,) + a, reads=2)

        def run(table):
            for name, *a in SCHED:
                if name in table:
                    table[name](*a)

        def cm(buf):
            return buf.rearrange("p (c t) -> p c t", t=CH)

        def c0(name, i=0, n=1):
            return chn[:, CHAN[name] + i:CHAN[name] + i + n]

        def d0(name, i=0, n=1):
            return der[:, DER[name] + i:DER[name] + i + n]

        sb_stages = [tuple(a) for name, *a in SCHED if name == "sb"]
        sb_units = [st + (j,) for st in sb_stages for j in sb_blocks(st[2])]
        sb_diags = [u for u in sb_units if u[3] >= 4 * u[2]]

        def sb_index(*unit_):
            return sb_units.index(unit_)

        def sb_diag_index(*unit_):
            return sb_diags.index(unit_)

        def so_before(*stage):
            return ("o",) + sb_stages[sb_stages.index(stage) - 1]

        def wait_av(eng, g):
            if g < 0:
                return
            if sb_units[g][3] == 0:
                so.rd_open(eng, ("o",) + sb_units[g][:3])
            else:
                eng.wait_ge(sem("av_done"), sum(u[3] != 0 for u in sb_units[:g + 1]))

        wides = [("o", n) for n in range(4)] + [("f", n) for n in range(4)]

        def wide_lo(m):
            return (vlo0, vlo1)[m % 2]

        def mixers_done(eng):
            eng.wait_ge(sem("conv_done"), 2)
            eng.wait_ge(sem("rw_done"), 2)
            eng.wait_ge(sem("h_done"), 2)
            so.wait_read(eng, ("o", 1, 1, 1))

        prob = [xa_scr[:, b * HALF:(b + 1) * HALF] for b in range(2)]
        probT = [xa_scr[:, (2 + b) * HALF:(3 + b) * HALF] for b in range(2)]
        amax = [xa_scr[:, 4 * HALF + 8 * b:4 * HALF + 8 * b + 8] for b in range(2)]

        shift_list = [tuple(t) for t in shifted]

        def gate_tile(kind):
            return {"rw": 0, "cv": 2, "h": 4, "s": 6}[kind[0]] + kind[1]

        def hlev_buf(l):
            return hz if l % 2 else hx

        def eps_ap(e):
            i = DER["eps"] + EPS.index(e)
            return der[:, i:i + 1]

        def dst_cols(dst):
            return int(dst.shape[-1])

        def kT_of(n):
            return kv[:, n // 4, (n % 4) * M:(n % 4 + 1) * M]

        def kv_vt(n):
            return B[:, 4, (n % 2) * M:(n % 2 + 1) * M]

        def v_of(n):
            return kv[:, 2:4, n * P:(n + 1) * P]

        hs = lambda h: slice(h * HALF, (h + 1) * HALF)
        rS, rC, ra, rk, rkk, rr, rv, rVt, rBt, rKt, rTT, rP1 = range(12)
        rL, rT = rS, rC
        rMak, rMrb, rMrk = rL, rT, rP1
        hx, hb, hq, hk, hz, hv_, hVt, hKt, hatt = range(9)

        block = ctx.enter_context(nc.Block())

        @block.sync
        def _(sp):
            sp.dma_start(fcst[:], fconst).then_inc(sem("consts_loaded"), 16)
            sp.dma_start(A[:, 6, 0:13 * CH], mconst).then_inc(sem("consts_loaded"), 16)
            sp.dma_start(chn[:], chan).then_inc(sem("consts_loaded"), 16)
            sp.dma_start(lora_sb[:], lora).then_inc(sem("consts_loaded"), 16)
            sp.dma_start(A[:, 4, :], norms[NORM_MIX:NORM_MIX + 1, :].broadcast_to([P, D])).then_inc(
                sem("consts_loaded"), 16)

            def load_x(i):
                if i >= 2:
                    sp.wait_ge(sem("x_scaled"), i - 1)
                sp.dma_start(A[:, i % 2, :], x[i * P:(i + 1) * P, :]).then_inc(sem(f"x_loaded{i % 2}"), 16)

            def load_w(n):
                kind = tiles[n]
                src, c = weight_columns(kind)
                for q in range(2):
                    m = 2 * n + q
                    if m >= 2:
                        sp.wait_ge(sem("w_split"), m - 1)
                    sp.dma_start(wraw[:, m % 2], wsrc[src][4 * P * q:4 * P * (q + 1), c:c + P].rearrange(
                        "(k p) n -> p k n", p=P)).then_inc(sem(f"w_loaded{m % 2}"), 16)

            for i in range(2):
                load_x(i)
            load_w(0)
            for i in range(2, TT):
                load_x(i)
            loaded_mem = False
            def load_wides(first):
                for m in range(first, first + 4):
                    src = {"o": w_out, "f": wo}[wides[m][0]]
                    c = wides[m][1] * 256
                    for q in range(4):
                        u = 4 * m + q
                        if u >= 2:
                            sp.wait_ge(sem("v_split"), u - 1)
                        else:
                            sp.wait_ge(sem("m_scaled"), 2)
                            so.wait_read(sp, ("o", 1, 1, 1))
                        sp.dma_start(vraw[:, u % 2], src[2 * P * q:2 * P * (q + 1), c:c + 256].rearrange(
                            "(k p) n -> p k n", p=P)).then_inc(sem(f"v_loaded{u % 2}"), 16)

            for n in range(1, len(tiles)):
                if tiles[n] == ["q", 0]:
                    mixers_done(sp)
                    sp.dma_start(x2[:, :, :], x.rearrange("(i p) d -> p i d", p=P)).then_inc(sem("x2_loaded"), 16)
                    load_wides(0)
                    sp.wait_ge(sem("y_split"), TT)
                    sp.dma_start(yT[:, 4, :], norms[NORM_X:NORM_X + 1, :].broadcast_to([P, D])).then_inc(
                        sem("gain_loaded"), 16)
                if tiles[n][0] == "mk" and not loaded_mem:
                    loaded_mem = True
                    so.wait_read(sp, ("o", 1, 1, 1))
                    for i in range(2):
                        sp.dma_start(B[:, 4 + i, :], mem[i * P:(i + 1) * P, :]).then_inc(sem("mem_loaded"), 16)
                    sp.dma_start(B[:, 6, :], norms[NORM_MEM:NORM_MEM + 1, :].broadcast_to([P, D])).then_inc(
                        sem("mem_loaded"), 16)
                load_w(n)
            load_wides(4)
            rw.rd_open(sp, ("ascore", TT - 1, 1))
            sp.dma_start(yT[:, 3, :], norms[NORM_FIN:NORM_FIN + 1, :].broadcast_to([P, D])).then_inc(
                sem("gain_loaded"), 16)
            for i in range(TT):
                sp.wait_ge(sem("out_ready"), i + 1)
                sp.dma_start(out[i * P:(i + 1) * P, :], yT[:, i % 2, :]).then_inc(sem(f"out_stored{i % 2}"), 16)
            for b in range(2):
                sp.wait_ge(sem(f"out_stored{b}"), 16 * TT // 2)

        @block.gpsimd
        def _(pool):
            nc.gpsimd.memset(raw[:, 0:1], 0.0).then_inc(sem("pool_init"), 1)
            nc.gpsimd.memset(reset[:], 1).then_inc(sem("pool_init"), 1)
            pool.wait_ge(sem("pool_init"), 2)
            nc.gpsimd.memset(reset[:, 0:T:CH], 0).then_inc(sem("pool_init"), 1)
            def split_wides(first):
                for m in range(first, first + 4):
                    for q in range(4):
                        u = 4 * m + q
                        pool.wait_ge(sem(f"v_loaded{u % 2}"), 16 * (u // 2 + 1))
                        if m >= 2:
                            pj.rd_open(pool, ("wide",) + wides[m - 2] + (TT - 1,))
                        elif q == 0:
                            mixers_done(pool)
                            pj.rd_open(pool, ("vtr", KT - 1))
                        hi, lo = vhi[:, m % 2, 2 * q:2 * q + 2, :], wide_lo(m)[:, 2 * q:2 * q + 2, :]
                        done(pool, nc.gpsimd.tensor_scalar(hi, vraw[:, u % 2], 1.0, 1.0, ALU.mult, ALU.mult), "v_hi")
                        done(pool, nc.gpsimd.tensor_tensor(lo, vraw[:, u % 2], hi.bitcast(F32), ALU.subtract),
                             "v_split")

            for n in range(len(tiles)):
                if tiles[n] == ["q", 0]:
                    split_wides(0)
                for q in range(2):
                    m = 2 * n + q
                    pool.wait_ge(sem(f"w_loaded{m % 2}"), 16 * (m // 2 + 1))
                    if n >= 2:
                        used = tuple(tiles[n - 2])
                        pj.rd_open(pool, used + (0 if used[0] in ("mk", "mv") else 1,))
                    hi, lo = whi[:, n % 2, 4 * q:4 * q + 4, :], wlo[:, n % 2, 4 * q:4 * q + 4, :]
                    done(pool, nc.gpsimd.tensor_scalar(hi, wraw[:, m % 2], 1.0, 1.0, ALU.mult, ALU.mult), "w_hi")
                    done(pool, nc.gpsimd.tensor_tensor(lo, wraw[:, m % 2], hi.bitcast(F32), ALU.subtract), "w_split")
            split_wides(4)

        @block.tensor
        def _(pe):
            mm, tr = nc.tensor.matmul, nc.tensor.transpose

            def transposed(name, src, i):
                for q in range(2):
                    bank = pj.pe_open(pe, (name, i, q))
                    for c in range(4):
                        k = 4 * q + c
                        ins = tr(bank[:, c * P:(c + 1) * P], src[:, k * P:(k + 1) * P], ident)
                    pj.pe_post(ins, (name, i, q))

            def xT(i):
                if i == 0:
                    pe.wait_ge(sem("consts_loaded"), 16 * N_CONSTS)
                pe.wait_ge(sem("x_scaled"), i + 1)
                transposed("xT", A[:, 2 + i % 2, :], i)

            def mT(i):
                pe.wait_ge(sem("m_scaled"), i + 1)
                transposed("mT", B[:, 4 + i, :], i)

            def hT(i):
                pe.wait_ge(sem("h_scaled"), i + 1)
                transposed("hT", yT[:, 6 + i % 2, :], i)

            def proj(*kind):
                n = tile_no[kind]
                small = kind[0] in ("mk", "mv")
                for h in range(1 if small else 2):
                    cols = slice(0, M) if small else hs(h)
                    if n == 0:
                        pj.wait_read(pe, ("xT", 4 * h + 3, 1))
                    if kind == ("mk", 0):
                        pj.wait_read(pe, ("mT", 1, 1))
                    if kind == ("q", 0):
                        pj.wait_read(pe, ("hT", 4 * h + 3, 1))
                    bank = pj.pe_open(pe, kind + (h,))[:, 0:cols.stop - cols.start]
                    for k in range(KT):
                        if h == 0 and k % 4 == 0:
                            pe.wait_ge(sem("w_split"), 2 * n + k // 4 + 1)
                        wh, wl = whi[:, n % 2, k, :], wlo[:, n % 2, k, :]
                        mm(bank, wh, act_hi[:, k, cols], start=k == 0, stop=False)
                        mm(bank, wh, act_lo[:, k, cols], start=False, stop=False)
                        ins = mm(bank, wl, act_hi[:, k, cols], start=False, stop=k == KT - 1)
                    pj.pe_post(ins, kind + (h,))

            def pairs(bank, h, lhsT, rhs, post, more=()):
                for c in range(8):
                    for hd in range(2):
                        r, col = slice(hd * HD, hd * HD + HD), slice((8 * h + c) * CH, (8 * h + c + 1) * CH)
                        terms = [(lhsT, rhs), *more]
                        for n, (a, b) in enumerate(terms):
                            ins = mm(bank[r, c * CH:(c + 1) * CH], a(r, col), b(r, col), start=n == 0,
                                     stop=n == len(terms) - 1)
                post(ins)

            def unit(ring, key):
                return ring.pe_open(pe, key), lambda ins: ring.pe_post(ins, key)

            def of(i):
                return lambda r, col: A[r, i, col]

            def lora_(p):
                pe.wait_ge(sem("xw_tanh"), 1)
                for w, r in (("z", slice(0, 32)), ("a", slice(32, 64))):
                    for h in range(2):
                        bank, post = unit(rw, (w, p, h))
                        post(mm(bank[:, :], lora_sb[r, p * P:(p + 1) * P], xm[r, hs(h)], start=True, stop=True))

            def block_sum(name, p, src, ready):
                for h in range(2):
                    ready(h)
                    bank, post = unit(rw, (name, p, h))
                    post(mm(bank[:, :], blk, src[:, hs(h)], start=True, stop=True))

            def kkn(p):
                block_sum("kkn", p, A[:, rP1, :], lambda h: pe.wait_ge(sem("kk_sq"), 2 * p + h + 1))

            def bon(p):
                block_sum("bon", p, A[:, rTT, :], lambda h: pe.wait_ge(sem("rk_ready"), p + 1))

            def tok(kind, p):
                src = {"v": A[:, rv], "b": A[:, ra], "k": A[:, rk], "hv": A[:, hatt], "hk": A[:, hk]}[kind]
                if kind == "v":
                    pe.wait_ge(sem("shift_done"), shift_no[("rw", p, "v")] + 1)
                elif kind in "bk":
                    pe.wait_ge(sem("bars_ready"), p + 1)
                elif kind == "hv":
                    for h in range(2):
                        pj.wait_read(pe, ("h", p, "i", h))
                else:
                    pe.wait_ge(sem("hk_ready"), p + 1)
                for h in range(2):
                    bank, post = unit(rw, ("tok", kind, p, h))
                    pairs(bank, h, lambda r, col: src[r, col], lambda r, col: ident[r, r], post)

            def minit(p):
                pe.wait_ge(sem("bars_ready"), p + 1)
                for h in range(2):
                    bank, post = unit(rw, ("L", p, h))
                    pairs(bank, h, of(rkk), of(ra), post)
                    bank, post = unit(rw, ("M", p, h))
                    pairs(bank, h, of(ra), of(rkk), post)

            def inv(p, l):
                for h in range(2):
                    if l == 1:
                        rw.wait_read(pe, ("M", p, h))
                    else:
                        rw.wait_read(pe, ("dT", p, l - 1, h))
                    bank, post = unit(rw, ("P1", p, l, h))
                    pairs(bank, h, of(rL), of(rTT), post)
                for h in range(2):
                    rw.wait_read(pe, ("P1", p, l, h))
                    bank, post = unit(rw, ("dTT", p, l, h))
                    pairs(bank, h, of(rT), of(rP1), post)
                if l < 5:
                    for h in range(2):
                        bank, post = unit(rw, ("dT", p, l, h))
                        pairs(bank, h, of(rP1), of(rT), post)

            def mk3(p):
                for w, a, b in (("ak", rk, rkk), ("rb", ra, rr), ("rk", rk, rr)):
                    for h in range(2):
                        bank, post = unit(rw, (w, p, h))
                        pairs(bank, h, of(a), of(b), post)

            def chunk(p, c):
                col = slice(c * CH, (c + 1) * CH)
                rs = [slice(0, HD), slice(HD, P)]
                if c == 0:
                    rw.wait_read(pe, ("rk", p, 1))
                    for kind in "vbk":
                        rw.wait_read(pe, ("tok", kind, p, 1))
                bank, post = unit(rw, ("R", p, c))
                if c == 1:
                    rw.wait_read(pe, ("S", p, 0))
                elif c:
                    pe.wait_ge(sem("state_ready"), p * (NC - 2) + c - 1)
                for r in rs:
                    ins = mm(bank[r, 0:CH], A[r, rMak, col], A[r, rVt, col], start=True, stop=c == 0)
                    if c:
                        ins = mm(bank[r, 0:CH], A[r, rkk, col], S_st[r, c % 2, :], start=False, stop=True)
                post(ins)
                rw.wait_read(pe, ("R", p, c))
                bank, post = unit(rw, ("U", p, c))
                for r in rs:
                    ins = mm(bank[r, 0:CH], A[r, rTT, col], R_sb[r, :], start=True, stop=True)
                post(ins)
                rw.wait_read(pe, ("U", p, c))
                if c < NC - 1:
                    bank, post = unit(rw, ("S", p, c))
                    for r in rs:
                        mm(bank[r, 0:CH], A[r, rKt, col], A[r, rVt, col], start=True, stop=False)
                        ins = mm(bank[r, 0:CH], A[r, rBt, col], U_sb[r, :], start=False, stop=True)
                    post(ins)
                bank, post = unit(rw, ("Y", p, c))
                for r in rs:
                    mm(bank[r, 0:CH], A[r, rVt, col], A[r, rMrk, col], start=True, stop=False)
                    ins = mm(bank[r, 0:CH], U_sb[r, :], A[r, rMrb, col], start=False, stop=c == 0)
                    if c:
                        ins = mm(bank[r, 0:CH], S_st[r, c % 2, :], A[r, rr, col], start=False, stop=True)
                post(ins)

            def mu(p):
                block_sum("mu", p, A[:, rkk, :], lambda h: rw.wait_read(pe, ("Y", p, 8 * h + 7)))

            def var(p):
                block_sum("var", p, A[:, rP1, :], lambda h: pe.wait_ge(sem("yc_sq"), 2 * p + h + 1))

            def cmean():
                pe.wait_ge(sem("conv_acc"), 1)
                for h in range(2):
                    bank, post = unit(rw, ("cmean", h))
                    mm(bank[:, :], negone, yT[:, 6, hs(h)], start=True, stop=False)
                    post(mm(bank[:, :], negone, yT[:, 7, hs(h)], start=False, stop=True))

            def cvar():
                for h in range(2):
                    pe.wait_ge(sem("conv_sq"), 2 * h + 2)
                    bank, post = unit(rw, ("cvar", h))
                    mm(bank[:, :], negone, yT[:, 4, hs(h)], start=True, stop=False)
                    post(mm(bank[:, :], negone, yT[:, 5, hs(h)], start=False, stop=True))

            def hdiag(p):
                pe.wait_ge(sem("hqk_ready"), p + 1)
                for h in range(2):
                    bank, post = unit(rw, ("hdiag", p, h))
                    pairs(bank, h, of(hk), of(hq), post)

            def hlev(p, l):
                for h in range(2):
                    pe.wait_ge(sem("hz_ready"), (6 * p + l) + 1)
                    bank, post = unit(rw, ("hl", p, l, h))
                    pairs(bank, h, of(hlev_buf(l)), of(hlev_buf(l)), post)

            def hkv(p):
                for h in range(2):
                    rw.wait_read(pe, ("tok", "hk", p, h))
                    bank, post = unit(rw, ("hkv", p, h))
                    pairs(bank, h, of(hKt), of(hVt), post)

            def hout(p):
                rw.wait_read(pe, ("hkv", p, 1))
                for h in range(2):
                    bank, post = unit(rw, ("hout", p, h))
                    pairs(bank, h, of(hVt), of(hatt), post, more=[(of(hz), of(hq))])

            def hvar(p):
                block_sum("hvar", p, A[:, hx, :], lambda h: pe.wait_ge(sem("ho_sq"), 2 * p + h + 1))

            def sv(p):
                for h in range(2):
                    pj.wait_read(pe, ("s", p, "v", h))
                for h in range(2):
                    bank = sz.pe_open(pe, ("sv", p, h))
                    for c in range(4):
                        ins = tr(bank[:, c * P:(c + 1) * P], B[:, 3, (4 * h + c) * P:(4 * h + c + 1) * P], ident)
                    sz.pe_post(ins, ("sv", p, h))

            def sb_(p, hd, th):
                r = slice(hd * HD, hd * HD + HD)
                blocks = sb_blocks(th)
                for h in range(2):
                    pj.wait_read(pe, ("s", p, "q", h))
                    pj.wait_read(pe, ("s", p, "k", h))
                    sz.wait_read(pe, ("sv", p, h))
                first = sb_index(p, hd, th, blocks[0])

                def z(j):
                    key = ("z", p, hd, th, j)
                    bank = sz.pe_open(pe, key)
                    a, n = sb_cols(th, j)
                    sz.pe_post(mm(bank[:, a:a + n], B[r, 1, j * P:(j + 1) * P], B[r, 0, th * HALF + a:th * HALF + a + n],
                                  start=True, stop=True), key)

                def tail(u, j):
                    key = ("z", p, hd, th, j)
                    bank = sz.bank(key)
                    a, n = sb_cols(th, j)
                    pe.wait_ge(sem("sp_ready"), first + u + 1)
                    spb = B[:, 4, (u % 2) * HALF:(u % 2) * HALF + HALF]
                    ins = mm(bank[:, a:a + n], tri, spb[:, a:a + n], start=False, stop=u == 0, skip_group_check=True)
                    if u:
                        rsb = B[:, 6, (u % 2) * HALF:(u % 2) * HALF + HALF]
                        a, n = sb_cols(th, j + 1)
                        ins = mm(bank[:, a:a + n], negone, rsb[:, a:a + n], start=False, stop=True,
                                 skip_group_check=True)
                    sz.pe_post(ins, key)

                def av(u, j):
                    a, n = sb_cols(th, j)
                    if u == 0:
                        so.pe_open(pe, ("o", p, hd, th))
                    if j >= 4 * th:
                        pe.wait_ge(sem("at_ready"), sb_diag_index(p, hd, th, j) + 1)
                    else:
                        sz.wait_read(pe, ("z", p, hd, th, j))
                    bank = so.bank(("o", p, hd, th))
                    atb = B[:, 5, (u % 2) * HALF:(u % 2) * HALF + HALF]
                    ins = mm(bank[r, a:a + n], B[:, 2, j * P + hd * HD:j * P + hd * HD + HD], atb[:, a:a + n],
                             start=u == 0, stop=j == 0, skip_group_check=True)
                    if j == 0:
                        so.pe_post(ins, ("o", p, hd, th))
                    else:
                        ins.then_inc(sem("av_done"), 1)

                z(blocks[0])
                for u, j in enumerate(blocks):
                    if u + 1 < len(blocks):
                        z(blocks[u + 1])
                    tail(u, j)
                    if u:
                        av(u - 1, blocks[u - 1])
                av(len(blocks) - 1, blocks[-1])

            def vtr(n):
                pj.wait_read(pe, ("mv", n, 0))
                bank = pj.pe_open(pe, ("vtr", n))
                for mi in range(2):
                    ins = tr(bank[:, mi * P:(mi + 1) * P], kv_vt(n)[:, mi * P:(mi + 1) * P], ident)
                pj.pe_post(ins, ("vtr", n))

            def wide(name, n, i):
                m = wides.index((name, n))
                tok_ = slice(i * P, (i + 1) * P)
                if n == 0:
                    if name == "o":
                        pe.wait_ge(sem("y_split"), i + 1)
                    else:
                        av_ring.wait_read(pe, ("aval", i, 1))
                key = ("wide", name, n, i)
                bank = pj.pe_open(pe, key)[:, 0:256]
                for k in range(KT):
                    if i == 0 and k % 2 == 0:
                        pe.wait_ge(sem("v_split"), 4 * m + k // 2 + 1)
                    ah, al = act_hi[:, k, tok_], act_lo[:, k, tok_]
                    mm(bank, ah, vhi[:, m % 2, k, :], start=k == 0, stop=False)
                    mm(bank, ah, wide_lo(m)[:, k, :], start=False, stop=False)
                    ins = mm(bank, al, vhi[:, m % 2, k, :], start=False, stop=k == KT - 1)
                pj.pe_post(ins, key)

            def ascore(i, g):
                if (i, g) == (0, 0):
                    for h in range(2):
                        pj.wait_read(pe, ("q", KT - 1, h))
                key = ("ascore", i, g)
                bank = rw.pe_open(pe, key)
                for e in range(2):
                    for d in range(2):
                        n = 4 * g + 2 * e + d
                        ins = mm(bank[:, e * M:(e + 1) * M], yT[:, n, i * P:(i + 1) * P], kT_of(n), start=d == 0,
                                 stop=d == 1)
                rw.pe_post(ins, key)

            def aturn(i, g):
                key = ("aturn", i, g)
                pe.wait_ge(sem("p_ready"), 2 * i + g + 1)
                bank = sz.pe_open(pe, key)
                for b in range(4):
                    ins = tr(bank[:, b * P:(b + 1) * P], prob[g][:, b * P:(b + 1) * P], ident)
                sz.pe_post(ins, key)

            def aval(i, g):
                key = ("aval", i, g)
                sz.wait_read(pe, ("aturn", i, g))
                bank = av_ring.pe_open(pe, key)
                for e in range(2):
                    for d in range(2):
                        n = 4 * g + 2 * e + d
                        o = bank[:, (2 * e + d) * P:(2 * e + d + 1) * P]
                        for mi in range(2):
                            ins = mm(o, kv[:, 2 + mi, n * P:(n + 1) * P],
                                     probT[g][:, (2 * e + mi) * P:(2 * e + mi + 1) * P], start=mi == 0, stop=mi == 1)
                av_ring.pe_post(ins, key)

            run({"xT": xT, "mT": mT, "proj": proj, "lora": lora_, "kkn": kkn, "bon": bon, "tok": tok, "minit": minit,
                 "inv": inv, "mk3": mk3, "chunk": chunk, "mu": mu, "var": var, "cmean": cmean, "cvar": cvar,
                 "hdiag": hdiag, "hlev": hlev, "hkv": hkv, "hout": hout, "hvar": hvar, "sv": sv, "sb": sb_,
                 "vtr": vtr, "hT": hT, "wide": wide, "ascore": ascore, "aturn": aturn, "aval": aval})

        @block.scalar
        def _(act):
            loaded = [None]

            def av(out, in_, func, **kw):
                want = {ACT.Exp: EXP_SET, ACT.Ln: EXP_SET, ACT.Sigmoid: SIG_SET, ACT.Tanh: SIG_SET}.get(func)
                if want and want != loaded[0]:
                    act.preload_act_table_set(want)
                    loaded[0] = want
                return nc.scalar.activation(out, in_, func, **kw)

            act.wait_ge(sem("lb_diff"), 1)
            done(act, av(d0("e", 0, 2), d0("e", 0, 2), ACT.Exp), "lb_exp")

            def exp(out, in_, name=None, scale=1.0, bias=0.0):
                done(act, av(out, in_, ACT.Exp, scale=scale, bias=bias), name or "act_step")

            def row_norm(src, junk, col):
                done(act, av(junk, src, ACT.Square, accum_out=stat[:, col:col + 1]), "act_step")
                done(act, av(stat[:, 32 + col:33 + col], stat[:, col:col + 1], ACT.Ln, scale=1.0 / D, bias=eps_ap(RMS_EPS)),
                     "act_step")
                exp(stat[:, 64 + col:65 + col], stat[:, 32 + col:33 + col], scale=-0.5, name="row_norm")

            def xn(i):
                if i == 0:
                    act.wait_ge(sem("derived"), 1)
                act.wait_ge(sem(f"x_loaded{i % 2}"), 16 * (i // 2 + 1))
                row_norm(A[:, i % 2, :], A[:, 5, :], i)

            def mn(i):
                act.wait_ge(sem("mem_loaded"), 48)
                row_norm(B[:, 4 + i, :], B[:, 2 + i, :], 8 + i)

            def hi_part(name, i):
                for q in range(2):
                    bank = pj.rd_open(act, (name, i, q))
                    pj.rd_done(act, nc.scalar.copy(act_hi[:, 4 * q:4 * q + 4, i * P:(i + 1) * P],
                                                   bank.rearrange("p (c t) -> p c t", c=4)), (name, i, q))

            def copy_out(ring, key, dst, scale=None, func=None, bias=None):
                bank = ring.rd_open(act, key)
                src = bank[:, 0:dst_cols(dst)]
                if func is not None:
                    ins = av(dst, src, func, bias=0.0 if bias is None else bias, scale=1.0 if scale is None else scale)
                elif scale is not None:
                    ins = nc.scalar.mul(dst, src, scale)
                else:
                    ins = nc.scalar.copy(dst, src)
                ring.rd_done(act, ins, key)

            def proj(*kind):
                n = tile_no[kind]
                g, what = kind[0], kind[-1]
                for h in range(1 if g in ("mk", "mv") else 2):
                    key = kind + (h,)
                    if kind in shift_list:
                        if h == 0:
                            if shift_no[kind]:
                                act.wait_ge(sem("shift_done"), shift_no[kind])
                            else:
                                act.wait_ge(sem("pool_init"), 3)
                        copy_out(pj, key, raw[:, 1 + h * HALF:1 + (h + 1) * HALF])
                    elif what == "gate":
                        y = gate_tile(kind)
                        if y >= 4:
                            act.wait_ge(sem("conv_done"), 2)
                        copy_out(pj, key, yT[:, y, hs(h)], func=ACT.Sigmoid)
                    elif g == "cv" and what == "glu":
                        copy_out(pj, key, yT[:, 4 + kind[1], hs(h)], func=ACT.Sigmoid)
                    elif g == "h":
                        if h == 0:
                            act.wait_ge(sem("rw_done"), 2)
                            if kind[1]:
                                act.wait_ge(sem("h_done"), kind[1])
                        if what == "q":
                            copy_out(pj, key, A[:, hq, hs(h)], func=ACT.Sigmoid)
                        elif what == "i":
                            copy_out(pj, key, A[:, hatt, hs(h)])
                        elif what == "f":
                            copy_out(pj, key, A[:, hz, hs(h)])
                            done(act, av(A[:, hx, hs(h)], A[:, hz, hs(h)], ACT.Sigmoid), "act_step")
                            done(act, av(A[:, hk, hs(h)], A[:, hz, hs(h)], ACT.Sigmoid, scale=-1.0), "hf_sig")
                    elif g == "s":
                        if kind[1] and h == 0:
                            so.wait_read(act, ("o", 0, 1, 1))
                        if what == "q":
                            copy_out(pj, key, B[:, 0, hs(h)], scale=HD ** -0.5)
                        elif what == "k":
                            copy_out(pj, key, B[:, 1, hs(h)])
                        elif what == "v":
                            copy_out(pj, key, B[:, 3, hs(h)])
                    elif g == "mk":
                        copy_out(pj, key, kT_of(kind[1]))
                    elif g == "mv":
                        if kind[1] >= 2:
                            pj.rd_open(act, ("vtr", kind[1] - 2))
                        copy_out(pj, key, kv_vt(kind[1]))
                    elif g == "q":
                        copy_out(pj, key, yT[:, kind[1], hs(h)], scale=float(D // 4) ** -0.5)

            def xwt():
                act.wait_ge(sem("shift_done"), shift_no[("xw",)] + 1)
                done(act, av(xm[0:32, :], xm[0:32, :], ACT.Tanh), "xw_tanh")

            def lora_(p):
                if p:
                    act.wait_ge(sem("rw_done"), p)
                for h in range(2):
                    copy_out(rw, ("z", p, h), A[:, rS, hs(h)], func=ACT.Sigmoid, bias=c0("w0", p))
                for h in range(2):
                    copy_out(rw, ("a", p, h), A[:, ra, hs(h)], func=ACT.Sigmoid, bias=c0("a0", p))

            def rwa(p):
                for h in range(2):
                    act.wait_ge(sem("kk_scaled"), p + 1)
                    done(act, av(A[:, rP1, hs(h)], A[:, rkk, hs(h)], ACT.Square), "kk_sq")
                act.wait_ge(sem("scan_done"), p + 1)
                exp(A[:, rBt, :], A[:, rC, :], scale=DECAY, name="e_incl")
                exp(A[:, rKt, :], A[:, rC, :], scale=-DECAY, name="e_neg")
                exp(DC[:, :], A[:, rC, CH - 1:T:CH], scale=DECAY, name="e_chunk")
                act.wait_ge(sem("s_excl"), p + 1)
                exp(A[:, rS, :], A[:, rS, :], scale=DECAY, name="e_excl")
                for h in range(2):
                    rw.wait_read(act, ("kkn", p, h))
                    done(act, av(A[:, rP1, hs(h)], A[:, rP1, hs(h)], ACT.Ln, scale=KK_SCALE), "act_step")
                    exp(A[:, rP1, hs(h)], A[:, rP1, hs(h)], scale=-0.5, name="kk_inv")

            def tok(kind, p):
                dst = {"v": rVt, "b": rBt, "k": rKt, "hv": hVt, "hk": hKt}[kind]
                for h in range(2):
                    copy_out(rw, ("tok", kind, p, h), A[:, dst, hs(h)])

            def minit(p):
                for h in range(2):
                    copy_out(rw, ("L", p, h), A[:, rL, hs(h)])

            def inv(p, l):
                for h in range(2):
                    copy_out(rw, ("P1", p, l, h), A[:, rP1, hs(h)])

            def chunk(p, c):
                copy_out(rw, ("R", p, c), R_sb[:, :])
                copy_out(rw, ("U", p, c), U_sb[:, :])
                copy_out(rw, ("Y", p, c), A[:, rkk, c * CH:(c + 1) * CH])

            def mu(p):
                for h in range(2):
                    rw.wait_read(act, ("mu", p, h))
                    done(act, av(A[:, rP1, hs(h)], A[:, rkk, hs(h)], ACT.Square), "yc_sq")

            def var(p):
                for h in range(2):
                    copy_out(rw, ("var", p, h), A[:, rTT, hs(h)], func=ACT.Ln, scale=1.0 / HD, bias=eps_ap(RWKV_EPS))
                    exp(A[:, rTT, hs(h)], A[:, rTT, hs(h)], scale=-0.5, name="y_rs")

            def csq():
                for h in range(2):
                    rw.wait_read(act, ("cmean", h))
                    for i in range(2):
                        done(act, av(yT[:, 4 + i, hs(h)], yT[:, 6 + i, hs(h)], ACT.Square), "conv_sq")

            def cvar():
                for h in range(2):
                    copy_out(rw, ("cvar", h), yT[:, 4, hs(h)], func=ACT.Ln, scale=-1.0 / G, bias=eps_ap(LN_EPS))
                    exp(yT[:, 4, hs(h)], yT[:, 4, hs(h)], scale=-0.5, name="conv_rs")

            def cfin():
                for i in range(2):
                    act.wait_ge(sem("conv_y"), i + 1)
                    done(act, av(yT[:, 5, :], yT[:, 6 + i, :], ACT.Sigmoid), "conv_sg")

            def hgate(p):
                act.wait_ge(sem("hf_floor"), p + 1)
                done(act, av(A[:, hx, :], A[:, hx, :], ACT.Ln, scale=d0("omlb", p), bias=d0("lb", p)), "hf_ln")

            def hlev(p, l):
                w, buf = 1 << l, A[:, hlev_buf(l), :].rearrange("p (b s w) -> p b s w", s=2, w=1 << l)
                act.wait_ge(sem("hdiff"), 6 * p + l + 1)
                exp(buf[:, :, 0, :], buf[:, :, 0, :], scale=-1.0)
                exp(buf[:, :, 1, :], buf[:, :, 1, :], name="hexp")

            def hbars(p):
                rw.wait_read(act, ("hl", p, 5, 1))
                exp(A[:, hz, :], A[:, hb, :], name="hq_exp")
                act.wait_ge(sem("hk_diff"), p + 1)
                exp(A[:, hx, :], A[:, hx, :], name="hk_exp")
                exp(DC[:, :], A[:, hb, CH - 1:T:CH], name="hdc")

            def hout(p):
                for h in range(2):
                    rw.wait_read(act, ("hout", p, h))
                    done(act, av(A[:, hx, hs(h)], A[:, hk, hs(h)], ACT.Square), "ho_sq")

            def hvar(p):
                for h in range(2):
                    copy_out(rw, ("hvar", p, h), A[:, hb, hs(h)], func=ACT.Ln, scale=1.0 / HD, bias=eps_ap(RMS_EPS))
                    exp(A[:, hb, hs(h)], A[:, hb, hs(h)], scale=-0.5, name="ho_rs")

            def sv(p):
                for h in range(2):
                    copy_out(sz, ("sv", p, h), B[:, 2, hs(h)])

            def sb_(p, hd, th):
                blocks = sb_blocks(th)
                first = sb_index(p, hd, th, blocks[0])

                def soft(u, j):
                    key = ("z", p, hd, th, j)
                    bank = sz.rd_open(act, key)
                    a, n = sb_cols(th, j)
                    e = B[:, 3, (u % 2) * HALF + a:(u % 2) * HALF + a + n]
                    if first + u >= 2:
                        act.wait_ge(sem("sp_ready"), first + u - 1)
                    if u < 2:
                        for h in range(2):
                            sz.wait_read(act, ("sv", p, h))
                    done(act, av(e, bank[:, a:a + n], ACT.Abs), "act_step")
                    exp(e, e, scale=-1.0)
                    done(act, av(e, e, ACT.Ln, bias=1.0), "sp_ln")

                def probs(u, j):
                    key = ("z", p, hd, th, j)
                    a, n = sb_cols(th, j)
                    at = B[:, 5, (u % 2) * HALF:(u % 2) * HALF + HALF]
                    bank = sz.bank(key)
                    diag = j >= 4 * th
                    if diag:
                        sz.wait_read(act, key, nth=1)
                        if n > P:
                            sz.rd_done(act, av(at[:, a + P:a + n], bank[:, a + P:a + n], ACT.Exp), key, nth=2)
                        exp(at[:, a:a + P], at[:, a:a + P], name="at_ready")
                    else:
                        sz.rd_open(act, key, post=2)
                        wait_av(act, first + u - 2)
                        sz.rd_done(act, av(at[:, a:a + n], bank[:, a:a + n], ACT.Exp), key)

                soft(0, blocks[0])
                for u, j in enumerate(blocks):
                    if u + 1 < len(blocks):
                        soft(u + 1, blocks[u + 1])
                    probs(u, j)

            def vtr(n):
                bank = pj.rd_open(act, ("vtr", n))
                pj.rd_done(act, nc.scalar.copy(v_of(n), bank[:, 0:M].rearrange("p (m v) -> p m v", m=2)), ("vtr", n))

            def ysplit(i):
                if i == 0:
                    mixers_done(act)
                    pj.rd_open(act, ("mv", KT - 1, 0))
                tok_ = slice(i * P, (i + 1) * P)
                done(act, nc.scalar.copy(act_hi[:, :, tok_], yT[:, :, tok_]), "y_hi")

            def x2n(i):
                if i == 0:
                    act.wait_ge(sem("y_split"), TT)
                pj.wait_read(act, ("wide", "o", 3, i))
                row_norm(x2[:, i, :], yT[:, 5, :], 10 + i)

            def fin(i):
                pj.wait_read(act, ("wide", "f", 3, i))
                row_norm(x2[:, i, :], yT[:, 2, :], 18 + i)

            def ascore(i, g):
                key = ("ascore", i, g)
                st_ = amax[g]
                rw.wait_read(act, key, nth=1)
                act.wait_ge(sem("a_max"), 2 * i + g + 1)
                for e in range(2):
                    src, dst = rw.bank(key)[:, e * M:(e + 1) * M], prob[g][:, e * M:(e + 1) * M]
                    ins = av(dst, src, ACT.Exp, bias=st_[:, e:e + 1], accum_out=st_[:, 2 + e:3 + e])
                    if e == 0:
                        done(act, ins, "act_step")
                    else:
                        rw.rd_done(act, ins, key, nth=2)

            def aturn(i, g):
                copy_out(sz, ("aturn", i, g), probT[g])

            def aval(i, g):
                key = ("aval", i, g)
                bank = av_ring.rd_open(act, key)
                av_ring.rd_done(act, nc.scalar.copy(act_hi[:, 4 * g:4 * g + 4, i * P:(i + 1) * P],
                                                    bank.rearrange("p (c t) -> p c t", c=4)), key)

            run({"xn": xn, "mn": mn, "xT": lambda i: hi_part("xT", i), "mT": lambda i: hi_part("mT", i), "proj": proj,
                 "xwt": xwt, "lora": lora_, "rwa": rwa, "tok": tok, "minit": minit, "inv": inv, "chunk": chunk,
                 "mu": mu, "var": var, "csq": csq, "cvar": cvar, "cfin": cfin, "hgate": hgate, "hlev": hlev,
                 "hbars": hbars, "hout": hout, "hvar": hvar, "sv": sv, "sb": sb_, "vtr": vtr,
                 "ysplit": ysplit, "x2n": x2n, "hT": lambda i: hi_part("hT", i), "ascore": ascore, "aturn": aturn,
                 "aval": aval, "fin": fin})

        @block.vector
        def _(dve):
            V = nc.vector

            def ok(ins, name="dve_step"):
                done(dve, ins, name)

            def tt(out, a, b, op, name="dve_step"):
                ok(V.tensor_tensor(out, a, b, op), name)

            def stt(out, a, s, b, op0, op1, name="dve_step"):
                ok(V.scalar_tensor_tensor(out=out, in0=a, scalar=s, in1=b, op0=op0, op1=op1), name)

            def ts(out, a, s1, s2, op0, op1=None, name="dve_step"):
                ok(V.tensor_scalar(out, a, s1, s2, op0, op1) if op1 is not None
                   else V.tensor_scalar(out, a, s1, None, op0), name)

            ADD, SUB, MUL, MAX, MIN = ALU.add, ALU.subtract, ALU.mult, ALU.max, ALU.min

            dve.wait_ge(sem("consts_loaded"), 16 * N_CONSTS)
            ok(V.tensor_copy(mcst[:], A[:, 6, 0:13 * CH]))
            ts(d0("omu", 0, 6), c0("mu", 0, 6), -1.0, 1.0, MUL, ADD)
            ts(d0("omux"), c0("mux"), -1.0, 1.0, MUL, ADD)
            ts(d0("oka", 0, 2), c0("k_a", 0, 2), -1.0, 1.0, MUL, ADD)
            tt(d0("e", 0, 2), c0("lbl", 0, 2), c0("lbl", 0, 2), SUB, "lb_diff")
            dve.wait_ge(sem("lb_exp"), 1)
            ok(V.reciprocal(d0("soft", 0, 2), d0("e", 0, 2)))
            tt(d0("soft", 0, 2), d0("soft", 0, 2), d0("e", 0, 2), MUL)
            tt(d0("lb", 0, 2), d0("soft", 0, 2), d0("soft", 0, 2), SUB)
            ts(d0("omlb", 0, 2), d0("lb", 0, 2), -1.0, 1.0, MUL, ADD)
            for n_, e_ in enumerate(EPS):
                ok(V.memset(der[:, DER["eps"] + n_:DER["eps"] + n_ + 1], e_),
                   "derived" if n_ == len(EPS) - 1 else "dve_step")

            def xn(i):
                dve.wait_ge(sem("row_norm"), i + 1)
                if i >= 2:
                    pj.rd_open(dve, ("xT", i - 2, 1))
                stt(A[:, 2 + i % 2, :], A[:, i % 2, :], stat[:, 64 + i:65 + i], A[:, 4, :], MUL, MUL, "x_scaled")

            def mn(i):
                dve.wait_ge(sem("row_norm"), TT + i + 1)
                stt(B[:, 4 + i, :], B[:, 4 + i, :], stat[:, 72 + i:73 + i], B[:, 6, :], MUL, MUL, "m_scaled")

            def lo_part(name, i):
                for q in range(2):
                    key = (name, i, q)
                    pj.wait_read(dve, key, nth=1)
                    dst = (slice(None), slice(4 * q, 4 * q + 4), slice(i * P, (i + 1) * P))
                    pj.rd_done(dve, V.tensor_tensor(act_lo[dst], pj.bank(key).rearrange("p (c t) -> p c t", c=4),
                                                    act_hi[dst].bitcast(F32), SUB), key, nth=2)

            def proj(*kind):
                g, what = kind[0], kind[-1]
                if kind in shift_list:
                    if g == "xw":
                        dst, mu_, omu_, r = xm[:, :], c0("mux"), d0("omux"), slice(0, 64)
                    else:
                        n = "rkv".index(what) * 2 + kind[1]
                        dst, mu_, omu_, r = A[:, {"r": rr, "k": rk, "v": rv}[what], :], c0("mu", n), d0("omu", n), \
                            slice(0, P)
                    for h in range(2):
                        pj.wait_read(dve, kind + (h,))
                    ts(dst, raw[r, 1:1 + T], omu_[r, :], None, MUL)
                    stt(dst, raw[r, 0:T], mu_[r, :], dst, MUL, ADD, "shift_done")
                elif what == "gate":
                    y = gate_tile(kind)
                    for h in range(2):
                        pj.wait_read(dve, kind + (h,), nth=1)
                        pj.rd_done(dve, V.tensor_tensor(yT[:, y, hs(h)], yT[:, y, hs(h)], pj.bank(kind + (h,)), MUL),
                                   kind + (h,), nth=2)
                elif g == "cv" and what == "val":
                    for h in range(2):
                        pj.wait_read(dve, ("cv", kind[1], "glu", h))
                        bank = pj.rd_open(dve, kind + (h,))
                        pj.rd_done(dve, V.tensor_tensor(yT[:, 4 + kind[1], hs(h)], yT[:, 4 + kind[1], hs(h)], bank,
                                                        MUL), kind + (h,))
                elif g == "h" and what == "q":
                    for h in range(2):
                        pj.wait_read(dve, kind + (h,), nth=1)
                        pj.rd_done(dve, V.tensor_tensor(A[:, hq, hs(h)], A[:, hq, hs(h)], pj.bank(kind + (h,)), MUL),
                                   kind + (h,), nth=2)

            def conv(i, part):
                lo, hi_ = part * CW // 4, (part + 1) * CW // 4
                for s in range(lo, hi_):
                    w = c0("cw", i * CW + CW - 1 - s)
                    u, acc = yT[:, 4 + i, 0:T - s], yT[:, 6 + i, s:T]
                    if s == 0:
                        ts(acc, u, w, c0("cb", i), MUL, ADD)
                    else:
                        stt(acc, u, w, acc, MUL, ADD, "conv_acc" if (i, s) == (1, CW - 1) else "dve_step")

            def cmean():
                for h in range(2):
                    bank = rw.rd_open(dve, ("cmean", h))
                    for i in range(2):
                        acc = yT[:, 6 + i, hs(h)]
                        rw.rd_done(dve, V.scalar_tensor_tensor(out=acc, in0=bank, scalar=1.0 / G, in1=acc, op0=MUL,
                                                               op1=ADD), ("cmean", h), nth=i + 1)

            def cfin():
                for i in range(2):
                    acc = yT[:, 6 + i, :]
                    if i == 0:
                        dve.wait_ge(sem("conv_rs"), 2)
                    stt(acc, acc, c0("cln_g", i), yT[:, 4, :], MUL, MUL)
                    ts(acc, acc, c0("cln_b", i), None, ADD, name="conv_y")
                    dve.wait_ge(sem("conv_sg"), i + 1)
                    tt(acc, acc, yT[:, 5, :], MUL)
                    tt(yT[:, 2 + i, :], yT[:, 2 + i, :], acc, MUL, "conv_done")

            def rwa(p):
                for h in range(2):
                    rw.wait_read(dve, ("z", p, h))
                    rw.wait_read(dve, ("a", p, h))
                ok(V.tensor_tensor_scan(A[:, rC, :], reset[:, :], A[:, rS, :], 0.0, MUL, ADD), "scan_done")
                tt(A[:, rS, :], A[:, rC, :], A[:, rS, :], SUB, "s_excl")
                ts(A[:, rkk, :], A[:, rk, :], c0("k_k", p), None, MUL, name="kk_scaled")
                ts(A[:, rTT, :], A[:, ra, :], c0("k_a", p), d0("oka", p), MUL, ADD)
                tt(A[:, rk, :], A[:, rk, :], A[:, rTT, :], MUL)
                stt(A[:, rTT, :], A[:, rr, :], c0("r_k", p), A[:, rk, :], MUL, MUL, "rk_ready")
                dve.wait_ge(sem("e_incl"), p + 1)
                tt(A[:, rr, :], A[:, rr, :], A[:, rBt, :], MUL)
                for h in range(2):
                    bank = rw.rd_open(dve, ("kkn", p, h))
                    rw.rd_done(dve, V.tensor_scalar(A[:, rP1, hs(h)], bank, 1e-24, None, MAX), ("kkn", p, h))

            def rwb(p):
                for h in range(2):
                    dve.wait_ge(sem("kk_inv"), 2 * p + h + 1)
                    stt(A[:, rkk, hs(h)], A[:, rP1, hs(h)], KK_SCALE ** 0.5, A[:, rkk, hs(h)], MUL, MUL)
                tt(A[:, ra, :], A[:, ra, :], A[:, rkk, :], MUL)
                dve.wait_ge(sem("e_neg"), p + 1)
                tt(A[:, ra, :], A[:, ra, :], A[:, rKt, :], MUL)
                tt(A[:, rk, :], A[:, rk, :], A[:, rKt, :], MUL)
                dve.wait_ge(sem("e_excl"), p + 1)
                stt(A[:, rkk, :], A[:, rkk, :], -1.0, A[:, rS, :], MUL, MUL, "bars_ready")

            def bon(p):
                rw.rd_open(dve, ("tok", "v", p, 1))
                for h in range(2):
                    bank = rw.rd_open(dve, ("bon", p, h))
                    rw.rd_done(dve, V.tensor_tensor(A[:, rv, hs(h)], A[:, rv, hs(h)], bank, MUL), ("bon", p, h))

            def chunks(ap):
                return ap.rearrange("p (c t) -> p c t", t=CH)

            def masked_copy(dst, mask, src):
                n = dst.shape[1] // CH
                return V.copy_predicated(chunks(dst), mask.unsqueeze(1).broadcast_to([P, n, CH]), chunks(src))

            def minit(p):
                eye = mcst[:, 12 * CH:13 * CH].unsqueeze(1).broadcast_to([P, NC, CH])
                ok(V.tensor_copy(cm(A[:, rTT, :]), eye))
                dve.wait_ge(sem("e_excl"), p + 1)
                ok(V.tensor_copy(cm(A[:, rT, :]), eye))
                for h in range(2):
                    rw.wait_read(dve, ("L", p, h), nth=1)
                    rw.rd_done(dve, masked_copy(A[:, rT, hs(h)], lev(6), rw.bank(("L", p, h))), ("L", p, h), nth=2)
                    bank = rw.rd_open(dve, ("M", p, h))
                    rw.rd_done(dve, masked_copy(A[:, rTT, hs(h)], lev(0), bank), ("M", p, h))

            def inv(p, l):
                for w, dst, m in (("dTT", rTT, l), ("dT", rT, 6 + l))[:2 if l < 5 else 1]:
                    for h in range(2):
                        bank = rw.rd_open(dve, (w, p, l, h))
                        rw.rd_done(dve, masked_copy(A[:, dst, hs(h)], lev(m), bank), (w, p, l, h))

            def mk3(p):
                for w, dst, m in (("ak", rMak, m_strict), ("rb", rMrb, m_incl), ("rk", rMrk, m_incl)):
                    for h in range(2):
                        bank = rw.rd_open(dve, (w, p, h))
                        rw.rd_done(dve, V.tensor_tensor(chunks(A[:, dst, hs(h)]), chunks(bank[:, :]),
                                                        m.unsqueeze(1).broadcast_to([P, 8, CH]), MUL), (w, p, h))

            def chunk(p, c):
                if c == NC - 1:
                    return
                s_old, s_new = S_st[:, c % 2, :], S_st[:, (c + 1) % 2, :]
                if c == 0:
                    dve.wait_ge(sem("e_chunk"), p + 1)
                bank = rw.rd_open(dve, ("S", p, c))
                if c == 0:
                    rw.rd_done(dve, V.tensor_scalar(s_new, bank[:, 0:CH], DC[:, c:c + 1], None, MUL), ("S", p, c))
                else:
                    rw.rd_done(dve, V.tensor_tensor(s_new, bank[:, 0:CH], s_old, ADD), ("S", p, c))
                    ts(s_new, s_new, DC[:, c:c + 1], None, MUL, name="state_ready")

            def mu(p):
                for h in range(2):
                    bank = rw.rd_open(dve, ("mu", p, h))
                    y = A[:, rkk, hs(h)]
                    rw.rd_done(dve, V.scalar_tensor_tensor(out=y, in0=bank, scalar=-1.0 / HD, in1=y, op0=MUL,
                                                           op1=ADD), ("mu", p, h))

            def rfin(p):
                dve.wait_ge(sem("y_rs"), 2 * p + 2)
                y = A[:, rkk, :]
                stt(y, y, c0("rln_g", p), A[:, rTT, :], MUL, MUL)
                stt(y, y, c0("rln_b", p), A[:, rv, :], ADD, ADD)
                tt(yT[:, p, :], yT[:, p, :], y, MUL, "rw_done")

            def hgate(p):
                dve.wait_ge(sem("hf_sig"), 2 * p + 2)
                ts(A[:, hx, :], A[:, hx, :], LN_FLOOR, None, MAX, name="hf_floor")
                ts(A[:, hk, :], A[:, hk, :], d0("omlb", p), None, MUL, name="hqk_ready")
                dve.wait_ge(sem("hf_ln"), p + 1)
                tt(A[:, hx, :], A[:, hx, :], A[:, hz, :], MIN)
                ok(V.tensor_tensor_scan(A[:, hb, :], reset[:, :], A[:, hx, :], 0.0, MUL, ADD))
                hdiff(p, 0)

            def hdiff(p, l):
                w = 1 << l
                b = A[:, hb, :].rearrange("p (b w) -> p b w", w=2 * w)
                o = A[:, hlev_buf(l), :].rearrange("p (b w) -> p b w", w=2 * w)
                tt(o, b, b[:, :, w - 1:w].broadcast_to([P, T // (2 * w), 2 * w]), SUB, "hdiff")

            def hdiag(p):
                rw.rd_open(dve, ("tok", "hv", p, 1))
                ok(V.memset(A[:, hatt, :], 0.0))
                for h in range(2):
                    bank = rw.rd_open(dve, ("hdiag", p, h))
                    rw.rd_done(dve, masked_copy(A[:, hatt, hs(h)], lev(12), bank), ("hdiag", p, h))

            def hlev_out(p, l):
                for h in range(2):
                    bank = rw.rd_open(dve, ("hl", p, l, h))
                    rw.rd_done(dve, masked_copy(A[:, hatt, hs(h)], lev(l), bank), ("hl", p, l, h))

            def hlev(p, l):
                v = lambda i: A[:, i, :].rearrange("p (b s w) -> p b s w", s=2, w=1 << l)
                buf = v(hlev_buf(l))
                dve.wait_ge(sem("hexp"), 6 * p + l + 1)
                tt(buf[:, :, 0, :], buf[:, :, 0, :], v(hk)[:, :, 0, :], MUL)
                tt(buf[:, :, 1, :], buf[:, :, 1, :], v(hq)[:, :, 1, :], MUL, "hz_ready")
                if l:
                    hlev_out(p, l - 1)
                if l < 5:
                    hdiff(p, l + 1)

            def hbars(p):
                hlev_out(p, 5)
                tt(cm(A[:, hx, :]), cm(A[:, hb, :])[:, :, CH - 1:CH].broadcast_to([P, NC, CH]), cm(A[:, hb, :]), SUB,
                   "hk_diff")
                dve.wait_ge(sem("hq_exp"), p + 1)
                tt(A[:, hq, :], A[:, hq, :], A[:, hz, :], MUL)
                dve.wait_ge(sem("hk_exp"), p + 1)
                tt(A[:, hk, :], A[:, hk, :], A[:, hx, :], MUL, "hk_ready")

            def hkv(p):
                s = cm(A[:, hz, :])
                ok(V.memset(s[:, 0, :], 0.0))
                dve.wait_ge(sem("hdc"), p + 1)
                for c in range(NC - 1):
                    key = ("hkv", p, c // 8)
                    bank = rw.rd_open(dve, key)
                    ins = V.scalar_tensor_tensor(out=s[:, c + 1, :], in0=s[:, c, :], scalar=DC[:, c:c + 1],
                                                 in1=bank[:, (c % 8) * CH:(c % 8 + 1) * CH], op0=MUL, op1=ADD)
                    if c in (7, NC - 2):
                        rw.rd_done(dve, ins, key)
                    else:
                        ok(ins)

            def hout(p):
                for h in range(2):
                    bank = rw.rd_open(dve, ("hout", p, h))
                    rw.rd_done(dve, V.tensor_copy(A[:, hk, hs(h)], bank), ("hout", p, h))

            def hfin(p):
                dve.wait_ge(sem("ho_rs"), 2 * p + 2)
                stt(A[:, hk, :], A[:, hk, :], c0("hn_g", p), A[:, hb, :], MUL, MUL)
                tt(yT[:, 4 + p, :], yT[:, 4 + p, :], A[:, hk, :], MUL, "h_done")

            def sb_(p, hd, th):
                blocks = sb_blocks(th)
                first = sb_index(p, hd, th, blocks[0])

                def soft(u, j):
                    key = ("z", p, hd, th, j)
                    bank = sz.bank(key)
                    a, n = sb_cols(th, j)
                    o = (u % 2) * HALF
                    if u >= 2:
                        sz.rd_open(dve, ("z", p, hd, th, blocks[u - 2]), post=2)
                    elif first:
                        so.rd_open(dve, so_before(p, hd, th))
                    if u:
                        q = ((u - 1) % 2) * HALF
                        a1, n1 = sb_cols(th, blocks[u - 1])
                        a2, n2 = sb_cols(th, blocks[u - 2]) if u > 1 else (a1 + n1, 0)
                        if n2:
                            tt(B[:, 6, o + a2:o + a2 + n2], B[:, 6, q + a2:q + a2 + n2], B[:, 4, q + a2:q + a2 + n2],
                               ADD)
                        if a2 > a1:
                            ok(V.tensor_copy(B[:, 6, o + a1:o + a2], B[:, 4, q + a1:q + a2]))
                    dve.wait_ge(sem("sp_ln"), first + u + 1)
                    diag = j >= 4 * th
                    stt(B[:, 4, o + a:o + a + n], bank[:, a:a + n], 0.0, B[:, 3, o + a:o + a + n], MAX, ADD,
                        "dve_step" if diag else "sp_ready")
                    if diag:
                        stt(B[:, 4, o + a:o + a + P], tri, 1.0, B[:, 4, o + a:o + a + P], ADD, MUL, "sp_ready")

                def probs(u, j):
                    if j < 4 * th:
                        return
                    key = ("z", p, hd, th, j)
                    a, n = sb_cols(th, j)
                    o = (u % 2) * HALF
                    bank = sz.rd_open(dve, key, post=2)
                    wait_av(dve, first + u - 2)
                    sz.rd_done(dve, V.scalar_tensor_tensor(out=B[:, 5, o + a:o + a + P], in0=tri, scalar=1e30,
                                                           in1=bank[:, a:a + P], op0=MUL, op1=ADD), key, nth=1)

                soft(0, blocks[0])
                for u, j in enumerate(blocks):
                    if u + 1 < len(blocks):
                        soft(u + 1, blocks[u + 1])
                    probs(u, j)
                key = ("o", p, hd, th)
                bank = so.rd_open(dve, key)
                r = slice(hd * HD, hd * HD + HD)
                so.rd_done(dve, V.tensor_tensor(yT[r, 6 + p, hs(th)], yT[r, 6 + p, hs(th)], bank[r, :], MUL), key)

            def ysplit(i):
                dve.wait_ge(sem("y_hi"), i + 1)
                tok_ = slice(i * P, (i + 1) * P)
                tt(act_lo[:, :, tok_], yT[:, :, tok_], act_hi[:, :, tok_].bitcast(F32), SUB, "y_split")

            def wide(name, n, i):
                key = ("wide", name, n, i)
                if (name, n, i) == ("o", 0, 0):
                    dve.wait_ge(sem("x2_loaded"), 16)
                bank = pj.rd_open(dve, key)
                dst = x2[:, i, n * 256:(n + 1) * 256]
                pj.rd_done(dve, V.tensor_tensor(dst, dst, bank[:, 0:256], ADD), key)

            def x2n(i):
                if i == 0:
                    dve.wait_ge(sem("gain_loaded"), 16)
                dve.wait_ge(sem("row_norm"), TT + 2 + i + 1)
                if i >= 2:
                    pj.rd_open(dve, ("hT", i - 2, 1))
                stt(yT[:, 6 + i % 2, :], x2[:, i, :], stat[:, 74 + i:75 + i], yT[:, 4, :], MUL, MUL, "h_scaled")

            def fin(i):
                if i == 0:
                    dve.wait_ge(sem("gain_loaded"), 32)
                dve.wait_ge(sem("row_norm"), 2 * TT + 2 + i + 1)
                if i >= 2:
                    dve.wait_ge(sem(f"out_stored{i % 2}"), 16 * (i // 2))
                stt(yT[:, i % 2, :], x2[:, i, :], stat[:, 82 + i:83 + i], yT[:, 3, :], MUL, MUL, "out_ready")

            def ascore(i, g):
                key = ("ascore", i, g)
                st_ = amax[g]
                if i:
                    sz.rd_open(dve, ("aturn", i - 1, g))
                bank = rw.rd_open(dve, key)
                rw.rd_done(dve, V.tensor_reduce(st_[:, 4:6], bank.rearrange("p (e m) -> p e m", e=2), AX.X, MAX), key,
                           nth=1)
                ts(st_[:, 0:2], st_[:, 4:6], -1.0, None, MUL, name="a_max")
                rw.wait_read(dve, key)
                ok(V.reciprocal(st_[:, 6:8], st_[:, 2:4]))
                for e in range(2):
                    pe_ = prob[g][:, e * M:(e + 1) * M]
                    ts(pe_, pe_, st_[:, 6 + e:7 + e], None, MUL, name="p_ready" if e else "dve_step")

            def aval(i, g):
                key = ("aval", i, g)
                av_ring.wait_read(dve, key, nth=1)
                dst = (slice(None), slice(4 * g, 4 * g + 4), slice(i * P, (i + 1) * P))
                av_ring.rd_done(dve, V.tensor_tensor(act_lo[dst], av_ring.bank(key).rearrange("p (c t) -> p c t", c=4),
                                                     act_hi[dst].bitcast(F32), SUB), key, nth=2)

            run({"xn": xn, "mn": mn, "xT": lambda i: lo_part("xT", i), "mT": lambda i: lo_part("mT", i), "proj": proj,
                 "conv": conv, "cmean": cmean, "cfin": cfin, "rwa": rwa, "rwb": rwb, "bon": bon, "minit": minit,
                 "inv": inv, "mk3": mk3, "chunk": chunk, "mu": mu, "rfin": rfin, "hgate": hgate, "hdiag": hdiag,
                 "hlev": hlev, "hbars": hbars, "hkv": hkv, "hout": hout, "hfin": hfin, "sb": sb_,
                 "ysplit": ysplit, "wide": wide, "x2n": x2n, "hT": lambda i: lo_part("hT", i), "ascore": ascore,
                 "aval": aval, "fin": fin})


_OUT = ((1, T, D), "float32")


def kernel(**inputs):
    import concourse.bacc as bacc
    from concourse import bass_utils

    v = {k: np.asarray(a) for k, a in inputs.items()}
    g2 = lambda a: a.reshape(-1, P).T
    chan = np.zeros((P, N_CHAN), np.float32)
    chan[:, CHAN["mu"]:CHAN["mu"] + 6] = g2(v["rwkv_mu"][0, :768])
    chan[:64, CHAN["mux"]] = v["rwkv_mu"][0, 768:]
    for name, src in (("w0", "rwkv_w0"), ("a0", "rwkv_a0"), ("k_k", "rwkv_k_k"), ("k_a", "rwkv_k_a"),
                      ("r_k", "rwkv_r_k"), ("rln_g", "rwkv_ln_g"), ("rln_b", "rwkv_ln_b"), ("cb", "conv_b"),
                      ("cln_g", "conv_ln_g"), ("cln_b", "conv_ln_b"), ("hn_g", "hgrn_norm_g"),
                      ("lbl", "hgrn_lb_logits")):
        chan[:, CHAN[name]:CHAN[name] + 2] = g2(v[src][0].reshape(G))
    chan[:, CHAN["cw"]:CHAN["cw"] + 2 * CW] = v["conv_w"][0].T.reshape(2, P, CW).transpose(1, 0, 2).reshape(P, 2 * CW)
    fconst, mconst = shape_constants()
    arrays = {
        "x": v["x"][0], "mem": v["mem"][0], "w_in": v["w_in"][0], "w_out": v["w_out"][0], "wq": v["xattn_wq"][0],
        "wk": v["xattn_wk"][0], "wv": v["xattn_wv"][0], "wo": v["xattn_wo"][0],
        "lora": np.concatenate([v["rwkv_w_up"][0], v["rwkv_a_up"][0]]),
        "chan": chan,
        "norms": np.stack([v["norm_mix"][0], v["norm_xattn"][0], v["norm_mem"][0], v["norm_final"]]),
        "fconst": fconst, "mconst": mconst,
    }
    nc = bacc.Bacc("TRN2", target_bir_lowering=False, num_devices=1)
    arrays = {f"in_{k}": np.ascontiguousarray(a) for k, a in arrays.items()}
    args = [nc.dram_tensor(k, a.shape, mybir.dt.from_np(a.dtype), kind="ExternalInput").ap()
            for k, a in arrays.items()]
    args.append(nc.dram_tensor("out_0", (T, D), F32, kind="ExternalOutput").ap())
    program(nc, *args)
    r = bass_utils.run_bass_kernel_spmd(nc, [arrays], core_ids=[0])
    return r.results[0]["out_0"].reshape(_OUT[0])
```

```python
from contextlib import ExitStack

import numpy as np

import concourse.bass as bass
from concourse import mybir

F32 = mybir.dt.float32
F32R = mybir.dt.float32r
U8 = mybir.dt.uint8
ALU = mybir.AluOpType
ACT = mybir.ActivationFunctionType
AX = mybir.AxisListType

P = 128
D = 1024
T = 1024
M = 256
KT = D // P
TT = T // P
G = 256
CH = 64
NC = T // CH
HD = 64
CW = 31
HALF = 512
RMS_EPS, LN_EPS, RWKV_EPS = 1e-6, 1e-5, 64e-5
DECAY = -float(np.exp(-0.5))
LN_FLOOR = 2.0 ** -63
KK_SCALE = 2.0 ** 16

C_R, C_K, C_V, C_XW, C_RG = 0, 256, 512, 768, 832
C_CV, C_CG, C_CGATE = 1088, 1344, 1600
C_HQ, C_HF, C_HI, C_HG = 1856, 2112, 2368, 2624
C_SQ, C_SK, C_SV, C_SG = 2880, 3136, 3392, 3648

CHAN = {}
_at = 0
for _n, _k in (("mu", 6), ("mux", 1), ("w0", 2), ("a0", 2), ("k_k", 2), ("k_a", 2), ("r_k", 2), ("rln_g", 2),
               ("rln_b", 2), ("cw", 2 * CW), ("cb", 2), ("cln_g", 2), ("cln_b", 2), ("hn_g", 2), ("lbl", 2)):
    CHAN[_n] = _at
    _at += _k
N_CHAN = _at
DER = {"omu": 0, "omux": 6, "oka": 7, "e": 9, "soft": 11, "lb": 13, "omlb": 15, "eps": 17}
N_DER = 24
NORM_MIX, NORM_X, NORM_MEM, NORM_FIN = range(4)
EPS = (RMS_EPS, LN_EPS, RWKV_EPS)
N_CONSTS = 3
EXP_SET = "natural_log_exp_and_others"
SIG_SET = "sigmoid_and_others"

SLACK, SLACK_OTHER = 0.4, 0.5
SUPPLY = 3.8
HOP = 0.15
HOLD = {
    ("sbz", 0, 0, 0, 0): ("cu", 1, 11), ("sbz", 0, 0, 1, 0): ("cu", 0, 9), ("sbz", 0, 1, 1, 0): ("cs", 1, 3),
    ("sbz", 1, 0, 0, 0): ("cu", 1, 8), ("sbz", 1, 0, 1, 0): ("cu", 0, 11),
    ("s", 0, "q"): ("rwa", 1), ("s", 1, "q"): ("cs", 1, 10),
    ("s", 1, "gate"): ("cr", 1, 8), ("h", 1, "gate"): ("cr", 1, 3), ("rw", 0, "gate"): ("invp", 0, 5, 1),
}
SMALL = ("tok", "minit", "invp", "invt", "mk3", "hdiag", "hlev", "hkv", "hout", "cr", "cu", "cs")
SMALL_RUN, SMALL_PER_PIECE = 1.0, 2.0


def sb_blocks(th):
    return list(range(4 * th + 3, -1, -1))


def sb_cols(th, j):
    a = max(j * P - th * HALF, 0)
    return a, HALF - a


def weight_columns(kind):
    g = kind[0]
    if g in ("mk", "mv", "q"):
        return {"mk": "wk", "mv": "wv", "q": "wq"}[g], kind[1] * P
    if g == "xw":
        return "w_in", C_XW
    first = {("rw", "r"): C_R, ("rw", "k"): C_K, ("rw", "v"): C_V, ("rw", "gate"): C_RG,
             ("cv", "val"): C_CV, ("cv", "glu"): C_CG, ("cv", "gate"): C_CGATE,
             ("h", "q"): C_HQ, ("h", "f"): C_HF, ("h", "i"): C_HI, ("h", "gate"): C_HG,
             ("s", "q"): C_SQ, ("s", "k"): C_SK, ("s", "v"): C_SV, ("s", "gate"): C_SG}[g, kind[2]]
    return "w_in", first + kind[1] * P


def mixer_chains():
    rec, stick, conv = [], [], []

    def proj(*kind):
        return ("proj",) + kind + (1,)

    def step(chain, stage, parts, *waits):
        chain.append((stage, parts, ([chain[-1][0]] if chain else []) + list(waits)))

    def halves(chain, stage, parts, waits=lambda h: None):
        before = [chain[-1][0]]
        for h in range(2):
            chain.append((stage + (h,), parts, before if waits(h) is None else waits(h)))

    step(rec, ("xwt",), [("AS", 1.1)], proj("xw"))
    for i in range(2):
        step(rec, ("lora", i), [("P", 3.4), ("AS", 2.2)])
        step(rec, ("rwa", i), [("D", 5.0), ("AE", 4.5, -1), ("D", 1.3)], proj("rw", i, "k"), proj("rw", i, "r"))
        step(rec, ("kkn", i), [("P", 1.8), ("D", 1.2), ("AE", 2.2)])
        step(rec, ("rwb", i), [("D", 6.2)])
        halves(rec, ("tok", "v", i), [("P", 1.3), ("A", 0.6)], lambda h: [proj("rw", i, "v")])
        step(rec, ("bon", i), [("P", 1.8), ("D", 1.2)])
        halves(rec, ("tok", "b", i), [("P", 1.3), ("A", 0.6)], lambda h: [("rwb", i)])
        halves(rec, ("tok", "k", i), [("P", 1.3), ("A", 0.6)], lambda h: [("rwb", i)])
        halves(rec, ("minit", i), [("D", 0.4), ("P", 2.6), ("A", 0.6, 1), ("D", 1.3)], lambda h: [("rwb", i)])
        for l in range(1, 6):
            halves(rec, ("invp", i, l), [("P", 1.3), ("A", 0.4)],
                   lambda h: [("invt", i, l - 1, h) if l > 1 else ("minit", i, h)])
            halves(rec, ("invt", i, l), [("P", 2.6), ("D", 0.8)] if l < 5 else [("P", 1.3), ("D", 0.4)],
                   lambda h: [("invp", i, l, h)])
        for w in ("ak", "rb", "rk"):
            halves(rec, ("mk3", w, i), [("P", 1.3), ("D", 0.7)], lambda h: [("invt", i, 5, h)])
        for c in range(NC):
            step(rec, ("cr", i, c), [("P", 0.35), ("A", 0.4)])
            step(rec, ("cu", i, c), [("P", 0.25), ("A", 0.4)])
            step(rec, ("cs", i, c), [("P", 0.9), ("A", 0.4), ("D", 0.4, 0)])
        step(rec, ("mu", i), [("P", 1.8), ("D", 1.3), ("A", 0.7)])
        step(rec, ("var", i), [("P", 1.8), ("AE", 2.2)])
        step(rec, ("rfin", i), [("D", 3.7)], proj("rw", i, "gate"))
    for i in range(2):
        step(rec, ("hgate", i), [("D", 1.4), ("AE", 1.1), ("D", 4.8)],
             proj("h", i, "f"), proj("h", i, "i"), proj("h", i, "q"))
        halves(rec, ("tok", "hv", i), [("P", 1.3), ("A", 0.6)], lambda h: [proj("h", i, "i")])
        halves(rec, ("hdiag", i), [("P", 1.3), ("D", 0.9)], lambda h: [("hgate", i)])
        for l in range(6):
            halves(rec, ("hlev", i, l), [("AE", 1.1), ("D", 0.8), ("P", 1.3), ("D", 1.0, 1)],
                   lambda h: [("hlev", i, l - 1, h) if l else ("hgate", i)])
        step(rec, ("hbars", i), [("AE", 1.1), ("D", 2.5), ("AE", 2.2), ("D", 2.5)], ("hlev", i, 5, 0))
        halves(rec, ("tok", "hk", i), [("P", 1.3), ("A", 0.6)])
        halves(rec, ("hkv", i), [("P", 1.3), ("D", 2.0)], lambda h: [("tok", "hk", i, h)])
        halves(rec, ("hout", i), [("P", 2.6), ("D", 0.7), ("A", 0.6)], lambda h: [("hkv", i, h)])
        step(rec, ("hvar", i), [("P", 1.8), ("AE", 2.2)])
        step(rec, ("hfin", i), [("D", 2.5)], proj("h", i, "gate"))

    for i in range(2):
        for tap in range(CW):
            step(conv, ("conv", i, tap), [("D", 1.25)], *[proj("cv", i, w) for w in ("glu", "val")])
    step(conv, ("cmean",), [("P", 3.4), ("D", 2.4)])
    step(conv, ("csq",), [("A", 2.1)])
    step(conv, ("cvar",), [("P", 3.4), ("AE", 2.2)])
    step(conv, ("cfin",), [("D", 3.0), ("AS", 2.2), ("D", 4.0)], proj("cv", 0, "gate"), proj("cv", 1, "gate"))

    for i in range(2):
        step(stick, ("sv", i), [("P", 0.6), ("A", 1.1)], *[proj("s", i, w) for w in "vqk"])
        for hd in range(2):
            for th in range(2):
                n = 4 * th + 4
                for u in range(-1, n + 1):
                    cols = lambda v: sb_cols(th, sb_blocks(th)[v])[1] / HALF
                    if u + 1 < n:
                        c = cols(u + 1)
                        step(stick, ("sbz", i, hd, th, u + 1), [("P", 0.85 * c), ("AE", 1.6 * c + 0.5), ("D", 1.3 * c)])
                    if 0 <= u < n:
                        c = cols(u)
                        step(stick, ("sbt", i, hd, th, u), [("P", 1.7 * c), ("AE", 0.6 * c + 0.2)])
                    if 1 <= u:
                        step(stick, ("sbv", i, hd, th, u - 1), [("P", 0.85 * cols(u - 1))])
                step(stick, ("sbo", i, hd, th), [("D", 0.8)], proj("s", i, "gate"))
    for n, (stage, parts, waits) in enumerate(stick):
        name, *a = stage
        if name in ("sbz", "sbt", "sbv"):
            p, hd, th, u = a
            first = [("sv", p)] if name == "sbz" else []
            follows = {"sbz": first + ([("sbt", p, hd, th, u - 2)] if u > 1 else []),
                       "sbt": [("sbz", p, hd, th, u)], "sbv": [("sbt", p, hd, th, u)]}[name]
            stick[n] = (stage, parts, follows)
    return rec, conv, stick


def mixer_order():
    rec, conv, stick = mixer_chains()
    tiles, needs = [], {}

    def want(*kind, after=()):
        tiles.append(kind)
        needs[kind] = list(after)

    for w in "krv":
        want("rw", 0, w)
    for i in range(2):
        want("cv", i, "glu")
        want("cv", i, "val")
    for w in "qkv":
        want("s", 0, w)
    for w in "krv":
        want("rw", 1, w, after=[("rfin", 0)])
    for w in "fqi":
        want("h", 0, w, after=[("rfin", 1)])
    for w in "fqi":
        want("h", 1, w, after=[("hfin", 0)])
    for w in "qkv":
        want("s", 1, w, after=[("sbo", 0, 1, 1)])
    want("rw", 0, "gate")
    for i in range(2):
        want("cv", i, "gate")
    for i in range(2):
        want("s", i, "gate", after=[("cfin",)])
    want("rw", 1, "gate")
    for i in range(2):
        want("h", i, "gate", after=[("cfin",)])
    all_in = [("proj",) + t + (1,) for t in tiles]
    needs[("xw",)] = []
    stick += [(("mn", 0), [("AE", 2.2), ("D", 1.3)], [("sbo", 1, 1, 1)]), (("mn", 1), [("AE", 2.2), ("D", 1.3)], []),
              (("mT", 0), [("P", 0.5), ("A", 1.1), ("D", 1.3)], [("mn", 0)] + all_in),
              (("mT", 1), [("P", 0.5), ("A", 1.1), ("D", 1.3)], [("mn", 1)])]
    for n in range(KT):
        want("mk", n, after=[("mT", 1)])
    for n in range(KT):
        want("mv", n, after=[("mT", 1)] + ([("vtr", n - 2)] if n >= 2 else []))
        stick.append((("vtr", n), [("P", 0.2), ("A", 0.4)], [("proj", "mv", n, 0)]))

    for chain in (conv, stick):
        for n, (stage, parts, waits) in enumerate(chain):
            if stage in HOLD:
                chain[n] = (stage, parts, list(waits) + [HOLD[stage]])
    for kind in tiles:
        if kind in HOLD:
            needs[kind].append(HOLD[kind])
    order, done, free = [], {}, {"P": 0.0, "A": 0.0, "D": 0.0, "table": "S"}

    def clocks(parts, waits):
        after, ends = dict(free), []
        ready, idle = max([done[w] for w in waits], default=0.0), 0.0
        for n, (eng, cost, *dep) in enumerate(parts):
            dep = dep[0] if dep else n - 1
            if len(eng) == 2:
                cost += 1.3 * (after["table"] != eng[1])
                eng, after["table"] = eng[0], eng[1]
            at = max(after[eng], (ready if dep < 0 else ends[dep]) + HOP)
            if eng == "P":
                idle += at - after[eng]
            after[eng] = at + cost
            ends.append(at + cost)
        return after, ends[-1], idle

    def put(stage, parts, waits=()):
        order.append(stage)
        after, done[stage], _ = clocks(parts, waits)
        free.update(after)

    chains, pieces = [list(rec), list(conv), list(stick)], [(("xw",), 1, k) for k in range(KT)]
    supplied, tile_over = -SUPPLY, [-SUPPLY, 0.0]
    small = 0.0
    while any(chains) or tiles or pieces:
        heads = []
        for c, chain in enumerate(chains):
            if chain and all(w in done for w in chain[0][2]):
                stage, parts, waits = chain[0]
                _, _, idle = clocks(parts, waits)
                if not any(p[0] == "P" for p in parts):
                    idle = max([done[w] for w in waits] + [free[parts[0][0][0]]]) - free["P"] - SLACK_OTHER
                elif stage[0] in SMALL and small >= SMALL_RUN:
                    idle = max(idle, 2 * SLACK)
                heads.append((idle, c))
        ok = [c for idle, c in heads if idle <= SLACK]
        if not pieces:
            ready = [t for t in tiles if all(w in done for w in needs[t])]
            if ready:
                kind = ready[0]
                tiles.remove(kind)
                pieces = [(kind, h, k) for h in range(1 if kind[0] in ("mk", "mv") else 2) for k in range(KT)]
        if ok or not pieces:
            stage, parts, waits = chains[ok[0] if ok else min(heads)[1]].pop(0)
            put(stage, parts, waits)
            if stage[0] in SMALL:
                small += sum(p[1] for p in parts if p[0] == "P")
        else:
            kind, h, k = pieces.pop(0)
            waits = needs[kind] if k == 0 else []
            if k == h == 0:
                done["weights"] = supplied = max(supplied, tile_over[-2]) + SUPPLY
                waits = waits + ["weights"]
            put(("piece",) + kind + (h, k), [("P", 0.32 if kind[0] in ("mk", "mv") else 0.64)], waits)
            small = max(0.0, small - SMALL_PER_PIECE)
            if k == KT - 1:
                g, what = kind[0], kind[-1]
                if what == "gate" or (g, what) == ("h", "q"):
                    parts = [("AS", 0.6), ("D", 0.7)]
                elif (g, what) == ("h", "f"):
                    parts = [("AS", 1.7)]
                elif (g, what) == ("cv", "glu"):
                    parts = [("AS", 0.6)]
                elif g in ("rw", "xw"):
                    parts = [("A", 0.6)] + [("D", 1.9)] * h
                elif (g, what) == ("cv", "val"):
                    parts = [("D", 0.7)]
                else:
                    parts = [("A", 0.6)]
                put(("proj",) + kind + (h,), parts, [("piece",) + kind + (h, k)])
                if not pieces:
                    tile_over.append(free["P"])
    return order


def schedule():
    s = [("xn", 0)]
    for i in range(TT):
        if i + 1 < TT:
            s.append(("xn", i + 1))
        s.append(("xT", i))
        if i == HALF // P:
            s += [("piece", "xw", 0, k) for k in range(KT)] + [("proj", "xw", 0)]
    s.append(("derive",))
    s += mixer_order()
    s += [("ysplit", i) for i in range(TT)]
    s += [("wide", "o", n, i) for n in range(3) for i in range(TT)]
    for i in range(TT + 2):
        if i < TT:
            s.append(("wide", "o", 3, i))
        if i > 1:
            s.append(("hT", i - 2))
        if i < TT:
            s.append(("x2n", i))
    for n in range(KT):
        for h in range(2):
            s += [("piece", "q", n, h, k) for k in range(KT)] + [("proj", "q", n, h)]
    at = [(i, g) for i in range(TT) for g in range(2)]
    for n in range(len(at) + 2):
        if n < len(at):
            s.append(("ascore",) + at[n])
        if 0 < n <= len(at):
            s.append(("aturn",) + at[n - 1])
        if n > 1:
            s.append(("aval",) + at[n - 2])
    s += [("wide", "f", n, i) for n in range(3) for i in range(TT)]
    for i in range(TT):
        s += [("wide", "f", 3, i), ("fin", i)]
    return s


def tiles_of(sched):
    return [a[:-1] for name, *a in sched if name == "proj" and a[-1] == 0]


def shape_constants():
    p = np.arange(P)
    f = np.zeros((P, 4 * P + 2 * CH), np.float32)
    f[:, 0:P] = np.eye(P)
    f[:, P:2 * P] = (p[:, None] // HD == p[None, :] // HD)
    f[:, 2 * P:3 * P] = -(p[:, None] >= p[None, :]).astype(np.float32)
    f[:, 3 * P:4 * P] = -1.0
    s, t = (p % CH)[:, None], np.arange(CH)[None, :]
    f[:, 4 * P:4 * P + CH] = s < t
    f[:, 4 * P + CH:] = s <= t
    m = np.zeros((P, 13 * CH), np.float32)
    for l in range(6):
        same = (s >> (l + 1)) == (t >> (l + 1))
        m[:, l * CH:(l + 1) * CH] = same & (((s >> l) & 1) == 0) & (((t >> l) & 1) == 1)
        m[:, (6 + l) * CH:(7 + l) * CH] = same & (((s >> l) & 1) == 1) & (((t >> l) & 1) == 0)
    m[:, 12 * CH:] = s == t
    return f, m


def program(nc, x, mem, w_in, w_out, wq, wk, wv, wo, lora, chan, norms, fconst, mconst, out):
    with ExitStack() as ctx:
        def sb(name, shape, dt=F32):
            return ctx.enter_context(nc.sbuf_tensor(name, shape, dt))

        act_hi = sb("act_hi", [P, KT, T], F32R)
        act_lo = sb("act_lo", [P, KT, T], F32R)
        yT = sb("yT", [P, KT, T])
        fcst = sb("fcst", [P, 4 * P + 2 * CH])
        mcst = sb("mcst", [P, 13 * CH], U8)
        chn = sb("chn", [P, N_CHAN])
        der = sb("der", [P, N_DER])
        lora_sb = sb("lora_sb", [64, G])
        reset = sb("reset", [P, T], U8)
        stat = sb("stat", [P, 96])
        S_st = sb("S_st", [P, 2, CH])
        S_dec = sb("S_dec", [P, CH])
        R_sb = sb("R_sb", [P, CH])
        U_sb = sb("U_sb", [P, CH])
        DC = sb("DC", [P, NC])
        ident = fcst[:, 0:P]
        blk = fcst[:, P:2 * P]
        tri = fcst[:, 2 * P:3 * P]
        negone = fcst[:, 3 * P:4 * P]
        m_strict = fcst[:, 4 * P:4 * P + CH]
        m_incl = fcst[:, 4 * P + CH:4 * P + 2 * CH]

        def lev(l):
            return mcst[:, l * CH:(l + 1) * CH]

        with ExitStack() as st:
            wraw = st.enter_context(nc.sbuf_tensor("wraw", [P, 2, 4, P], F32))
            whi = st.enter_context(nc.sbuf_tensor("whi", [P, 2, KT, P], F32R))
            wlo = st.enter_context(nc.sbuf_tensor("wlo", [P, 2, KT, P], F32R))
        xa_scr = sb("xa_scr", [P, 5 * T])
        with ExitStack() as st:
            A = st.enter_context(nc.sbuf_tensor("A", [P, 12, T], F32))
            raw = st.enter_context(nc.sbuf_tensor("raw", [P, 1 + T], F32))
            xm = st.enter_context(nc.sbuf_tensor("xm", [64, T], F32))
            B = st.enter_context(nc.sbuf_tensor("B", [P, 7, T], F32))
        with ExitStack() as st:
            x2 = st.enter_context(nc.sbuf_tensor("x2", [P, TT, D], F32))
            vhi = st.enter_context(nc.sbuf_tensor("vhi", [P, 2, KT, 256], F32R))
            vlo0 = st.enter_context(nc.sbuf_tensor("vlo0", [P, KT, 256], F32R))
            _gap = st.enter_context(nc.sbuf_tensor("gap", [P, 1], F32))
            kv = st.enter_context(nc.sbuf_tensor("kv", [P, 4, T], F32))
            vlo1 = st.enter_context(nc.sbuf_tensor("vlo1", [P, KT, 256], F32R))
            vraw = st.enter_context(nc.sbuf_tensor("vraw", [P, 2, 2, 256], F32))

        banks = [ctx.enter_context(nc.psum_tensor(f"bank{i}", [P, HALF], F32)) for i in range(8)]

        sems, counts = {}, {}

        def sem(name):
            if name not in sems:
                sems[name] = ctx.enter_context(nc.semaphore(name))
            return sems[name]

        def done(eng, ins, name):
            counts[name] = counts.get(name, 0) + 1
            ins.then_inc(sem(name), 1)
            eng.wait_ge(sem(name), counts[name])

        class Ring:

            def __init__(self, name, ids):
                self.name, self.ids, self.units, self.n = name, ids, {}, 0
                self.posted, self.read = [0] * len(ids), [0] * len(ids)

            def plan(self, key, reads=1, posts=1):
                b = self.n % len(self.ids)
                self.units[key] = (b, self.posted[b], self.read[b], reads)
                self.n += 1
                self.posted[b] += posts
                self.read[b] += reads

            def bank(self, key):
                return banks[self.ids[self.units[key][0]]][:, :]

            def ready(self, b):
                return sem(f"{self.name}{b}_ready")

            def free(self, b):
                return sem(f"{self.name}{b}_free")

            def pe_open(self, pe, key):
                b, _, r, _ = self.units[key]
                if r:
                    pe.wait_ge(self.free(b), r)
                return self.bank(key)

            def pe_post(self, ins, key):
                ins.then_inc(self.ready(self.units[key][0]), 1)

            def rd_open(self, eng, key, post=1):
                b, n, _, _ = self.units[key]
                eng.wait_ge(self.ready(b), n + post)
                return self.bank(key)

            def rd_done(self, eng, ins, key, nth=1):
                b, _, r, _ = self.units[key]
                ins.then_inc(self.free(b), 1)
                eng.wait_ge(self.free(b), r + nth)

            def wait_read(self, eng, key, nth=None):
                b, _, r, k = self.units[key]
                eng.wait_ge(self.free(b), r + (k if nth is None else nth))

        pj = Ring("pj", [0, 1, 2])
        rw = Ring("rw", [3, 4])
        sz = Ring("sz", [5, 6])
        so = Ring("so", [7])
        av_ring = so

        SCHED = schedule()
        raw_slots, raw_last, raw_plan = [wraw[:, 0], wraw[:, 1], B[:, 5, 0:HALF], B[:, 5, HALF:T]], {}, []
        for t in tiles_of(SCHED):
            for q in range(2):
                m = len(raw_plan)
                if t[0] in ("mk", "mv"):
                    slot = min(range(4), key=lambda s: raw_last.get(s, (-1, 0))[0])
                else:
                    slot = min(range(2), key=lambda s: raw_last.get(s, (-1, 0))[0])
                before, loads = raw_last.get(slot, (None, 0))
                raw_last[slot] = (m, loads + 1)
                raw_plan.append((slot, before, loads + 1))
        raw_view = [r if n < 2 else r.rearrange("p (k n) -> p k n", n=P) for n, r in enumerate(raw_slots)]
        wsrc = {"w_in": w_in, "wk": wk, "wv": wv, "wq": wq}
        tiles = tiles_of(SCHED)
        tile_no = {tuple(t): n for n, t in enumerate(tiles)}
        shifted = [t for t in tiles if t[0] == "xw" or (t[0] == "rw" and t[2] in "rkv")]
        shift_no = {tuple(t): n for n, t in enumerate(shifted)}
        for name, *a in SCHED:
            a = tuple(a)
            if name in ("xT", "mT", "hT"):
                for q in range(2):
                    pj.plan((name,) + a + (q,), reads=2)
            elif name == "piece":
                if a[-1] == 0:
                    pj.plan(a[:-1], reads=2 if a[-3] == "gate" or (a[0], a[-3]) == ("h", "q") else 1)
            elif name == "lora":
                for w in "za":
                    for h in range(2):
                        rw.plan((w,) + a + (h,))
            elif name in ("kkn", "bon", "mu", "var", "hvar"):
                for h in range(2):
                    rw.plan((name,) + a + (h,))
            elif name in ("tok", "hdiag", "hlev", "hkv", "hout"):
                rw.plan((name,) + a)
            elif name == "minit":
                rw.plan(("L",) + a, reads=2)
                rw.plan(("M",) + a)
            elif name == "invp":
                rw.plan(("P1",) + a)
            elif name == "invt":
                for w in ("dTT", "dT")[:2 if a[1] < 5 else 1]:
                    rw.plan((w,) + a)
            elif name == "mk3":
                rw.plan(a)
            elif name in ("cr", "cu"):
                rw.plan(({"cr": "R", "cu": "U"}[name],) + a)
            elif name == "cs":
                for w in ("S", "Y") if a[1] < NC - 1 else ("Y",):
                    rw.plan((w,) + a)
            elif name in ("cmean", "cvar"):
                for h in range(2):
                    rw.plan((name, h), reads=2 if name == "cmean" else 1)
            elif name == "sv":
                for h in range(2):
                    sz.plan((name,) + a + (h,))
            elif name == "sbz":
                p, hd, th, u = a
                j = sb_blocks(th)[u]
                sz.plan(("z", p, hd, th, j), reads=2 if j >= 4 * th and sb_cols(th, j)[1] > P else 1, posts=2)
                if u == 0:
                    so.plan(("o", p, hd, th))
            elif name in ("vtr", "wide"):
                pj.plan((name,) + a)
            elif name == "ascore":
                rw.plan((name,) + a, reads=2)
            elif name == "aturn":
                sz.plan((name,) + a)
            elif name == "aval":
                av_ring.plan((name,) + a, reads=2)

        def run(table):
            for name, *a in SCHED:
                if name in table:
                    table[name](*a)

        def cm(buf):
            return buf.rearrange("p (c t) -> p c t", t=CH)

        def level_half(ap, l, bit):
            return ap.rearrange("p (b s w) -> p b s w", s=2, w=1 << l)[:, :, bit, :]

        def c0(name, i=0, n=1):
            return chn[:, CHAN[name] + i:CHAN[name] + i + n]

        def d0(name, i=0, n=1):
            return der[:, DER[name] + i:DER[name] + i + n]

        sb_stages = [tuple(a) for name, *a in SCHED if name == "sbo"]
        sb_units = [st + (j,) for st in sb_stages for j in sb_blocks(st[2])]
        sb_diags = [u for u in sb_units if u[3] >= 4 * u[2]]

        def sb_index(*unit_):
            return sb_units.index(unit_)

        def sb_diag_index(*unit_):
            return sb_diags.index(unit_)

        def so_before(*stage):
            return ("o",) + sb_stages[sb_stages.index(stage) - 1]

        def wait_av(eng, g):
            if g < 0:
                return
            if sb_units[g][3] == 0:
                so.rd_open(eng, ("o",) + sb_units[g][:3])
            else:
                eng.wait_ge(sem("av_done"), sum(u[3] != 0 for u in sb_units[:g + 1]))

        wides = [("o", n) for n in range(4)] + [("f", n) for n in range(4)]

        def wide_lo(m):
            return (vlo0, vlo1)[m % 2]

        def mixers_done(eng):
            eng.wait_ge(sem("conv_done"), 2)
            eng.wait_ge(sem("rw_done"), 2)
            eng.wait_ge(sem("h_done"), 2)
            so.wait_read(eng, ("o", 1, 1, 1))

        prob = [xa_scr[:, b * HALF:(b + 1) * HALF] for b in range(2)]
        probT = [xa_scr[:, (2 + b) * HALF:(3 + b) * HALF] for b in range(2)]
        amax = [xa_scr[:, 4 * HALF + 8 * b:4 * HALF + 8 * b + 8] for b in range(2)]

        shift_list = [tuple(t) for t in shifted]

        def gate_tile(kind):
            return {"rw": 0, "cv": 2, "h": 4, "s": 6}[kind[0]] + kind[1]

        def hlev_buf(l):
            return hz if l % 2 else hx

        def eps_ap(e):
            i = DER["eps"] + EPS.index(e)
            return der[:, i:i + 1]

        def dst_cols(dst):
            return int(dst.shape[-1])

        def kT_of(n):
            return kv[:, n // 4, (n % 4) * M:(n % 4 + 1) * M]

        def kv_vt(n):
            return B[:, 4, (n % 2) * M:(n % 2 + 1) * M]

        def v_of(n):
            return kv[:, 2:4, n * P:(n + 1) * P]

        hs = lambda h: slice(h * HALF, (h + 1) * HALF)
        rS, rC, ra, rk, rkk, rr, rv, rVt, rBt, rKt, rTT, rP1 = range(12)
        rL, rT = rS, rC
        rMak, rMrb, rMrk = rL, rT, rP1
        hx, hb, hq, hk, hz, hv_, hVt, hKt, hatt = range(9)

        block = ctx.enter_context(nc.Block())

        @block.sync
        def _(sp):
            def load_x(i):
                if i >= 2:
                    sp.wait_ge(sem("x_scaled"), i - 1)
                sp.dma_start(A[:, i % 2, :], x[i * P:(i + 1) * P, :]).then_inc(sem(f"x_loaded{i % 2}"), 16)

            def load_w(n):
                kind = tiles[n]
                src, c = weight_columns(kind)
                for q in range(2):
                    slot, before, _ = raw_plan[2 * n + q]
                    if before is not None:
                        sp.wait_ge(sem("w_split"), before + 1)
                    elif slot >= 2:
                        pj.rd_open(sp, ("mT", 1, 1))
                    sp.dma_start(raw_view[slot], wsrc[src][4 * P * q:4 * P * (q + 1), c:c + P].rearrange(
                        "(k p) n -> p k n", p=P)).then_inc(sem(f"w_loaded{slot}"), 16)

            load_x(0)
            sp.dma_start(A[:, 4, :], norms[NORM_MIX:NORM_MIX + 1, :].broadcast_to([P, D])).then_inc(
                sem("mix_gain_loaded"), 16)
            sp.dma_start(fcst[:], fconst).then_inc(sem("ident_loaded"), 16)
            load_x(1)
            load_x(2)
            load_w(0)
            for i in range(3, TT):
                load_x(i)
            sp.dma_start(A[:, 6, 0:13 * CH], mconst).then_inc(sem("consts_loaded"), 16)
            sp.dma_start(chn[:], chan).then_inc(sem("consts_loaded"), 16)
            sp.dma_start(lora_sb[:], lora).then_inc(sem("consts_loaded"), 16)
            loaded_mem = False

            def load_wides(first, last):
                for m in range(first, last):
                    src = {"o": w_out, "f": wo}[wides[m][0]]
                    c = wides[m][1] * 256
                    for q in range(4):
                        u = 4 * m + q
                        if u >= 2:
                            sp.wait_ge(sem("v_split"), u - 1)
                        else:
                            sp.wait_ge(sem("m_scaled"), 2)
                            so.wait_read(sp, ("o", 1, 1, 1))
                        sp.dma_start(vraw[:, u % 2], src[2 * P * q:2 * P * (q + 1), c:c + 256].rearrange(
                            "(k p) n -> p k n", p=P)).then_inc(sem(f"v_loaded{u % 2}"), 16)

            for n in range(1, len(tiles)):
                if tiles[n] == ["q", 0]:
                    load_wides(0, 1)
                    mixers_done(sp)
                    for i in range(TT):
                        sp.dma_start(x2[:, i, :], x[i * P:(i + 1) * P, :]).then_inc(sem(f"x2_loaded{i}"), 16)
                    load_wides(1, 4)
                    sp.wait_ge(sem("y_split"), TT)
                    sp.dma_start(yT[:, 4, :], norms[NORM_X:NORM_X + 1, :].broadcast_to([P, D])).then_inc(
                        sem("gain_loaded"), 16)
                if tiles[n][0] == "mk" and not loaded_mem:
                    loaded_mem = True
                    so.wait_read(sp, ("o", 1, 1, 1))
                    for i in range(2):
                        sp.dma_start(B[:, 4 + i, :], mem[i * P:(i + 1) * P, :]).then_inc(sem("mem_loaded"), 16)
                    sp.dma_start(B[:, 6, :], norms[NORM_MEM:NORM_MEM + 1, :].broadcast_to([P, D])).then_inc(
                        sem("mem_loaded"), 16)
                load_w(n)
            load_wides(4, 8)
            rw.rd_open(sp, ("ascore", TT - 1, 1))
            sp.dma_start(yT[:, 3, :], norms[NORM_FIN:NORM_FIN + 1, :].broadcast_to([P, D])).then_inc(
                sem("gain_loaded"), 16)
            for i in range(TT):
                sp.wait_ge(sem("out_ready"), i + 1)
                sp.dma_start(out[i * P:(i + 1) * P, :], yT[:, i % 2, :]).then_inc(sem(f"out_stored{i % 2}"), 16)
            for b in range(2):
                sp.wait_ge(sem(f"out_stored{b}"), 16 * TT // 2)

        @block.gpsimd
        def _(pool):
            nc.gpsimd.memset(raw[:, 0:1], 0.0).then_inc(sem("pool_init"), 1)
            nc.gpsimd.memset(reset[:], 1).then_inc(sem("pool_init"), 1)
            pool.wait_ge(sem("pool_init"), 2)
            nc.gpsimd.memset(reset[:, 0:T:CH], 0).then_inc(sem("pool_init"), 1)

            def split_wides(first):
                for m in range(first, first + 4):
                    for q in range(4):
                        u = 4 * m + q
                        pool.wait_ge(sem(f"v_loaded{u % 2}"), 16 * (u // 2 + 1))
                        if m >= 2:
                            pj.rd_open(pool, ("wide",) + wides[m - 2] + (TT - 1,))
                        elif q == 0 and m == 0:
                            pool.wait_ge(sem("rw_done"), 2)
                        elif q == 0:
                            mixers_done(pool)
                            pj.rd_open(pool, ("vtr", KT - 1))
                        hi, lo = vhi[:, (m + 1) % 2, 2 * q:2 * q + 2, :], wide_lo(m)[:, 2 * q:2 * q + 2, :]
                        done(pool, nc.gpsimd.tensor_scalar(hi, vraw[:, u % 2], 1.0, 1.0, ALU.mult, ALU.mult), "v_hi")
                        done(pool, nc.gpsimd.tensor_tensor(lo, vraw[:, u % 2], hi.bitcast(F32), ALU.subtract),
                             "v_split")

            for n in range(len(tiles)):
                if tiles[n] == ["q", 0]:
                    split_wides(0)
                for q in range(2):
                    slot, _, loads = raw_plan[2 * n + q]
                    pool.wait_ge(sem(f"w_loaded{slot}"), 16 * loads)
                    if n >= 2:
                        used = tuple(tiles[n - 2])
                        pj.rd_open(pool, used + (0 if used[0] in ("mk", "mv") else 1,))
                    hi, lo = whi[:, n % 2, 4 * q:4 * q + 4, :], wlo[:, n % 2, 4 * q:4 * q + 4, :]
                    done(pool, nc.gpsimd.tensor_scalar(hi, raw_view[slot], 1.0, 1.0, ALU.mult, ALU.mult), "w_hi")
                    done(pool, nc.gpsimd.tensor_tensor(lo, raw_view[slot], hi.bitcast(F32), ALU.subtract), "w_split")
            split_wides(4)

        @block.tensor
        def _(pe):
            mm, tr = nc.tensor.matmul, nc.tensor.transpose
            heads = [slice(0, HD), slice(HD, P)]

            def transposed(name, src, i):
                for q in range(2):
                    bank = pj.pe_open(pe, (name, i, q))
                    for c in range(4):
                        k = 4 * q + c
                        ins = tr(bank[:, c * P:(c + 1) * P], src[:, k * P:(k + 1) * P], ident)
                    pj.pe_post(ins, (name, i, q))

            def xT(i):
                if i == 0:
                    pe.wait_ge(sem("ident_loaded"), 16)
                pe.wait_ge(sem("x_scaled"), i + 1)
                transposed("xT", A[:, 2 + i % 2, :], i)

            def mT(i):
                pe.wait_ge(sem("m_scaled"), i + 1)
                transposed("mT", B[:, 4 + i, :], i)

            def hT(i):
                pe.wait_ge(sem("h_scaled"), i + 1)
                transposed("hT", yT[:, 6 + i % 2, :], i)

            def piece(*a):
                *kind, h, k = a
                kind = tuple(kind)
                n = tile_no[kind]
                cols = slice(0, M) if kind[0] in ("mk", "mv") else hs(h)
                key = kind + (h,)
                if k == 0:
                    if n == 0:
                        pj.wait_read(pe, ("xT", 4 * h + 3, 1))
                    if kind == ("mk", 0):
                        pj.wait_read(pe, ("mT", 1, 1))
                    if kind == ("q", 0):
                        pj.wait_read(pe, ("hT", 4 * h + 3, 1))
                    pj.pe_open(pe, key)
                bank = pj.bank(key)[:, 0:cols.stop - cols.start]
                if h == 0 and k % 4 == 0:
                    pe.wait_ge(sem("w_split"), 2 * n + k // 4 + 1)
                wh, wl = whi[:, n % 2, k, :], wlo[:, n % 2, k, :]
                mm(bank, wh, act_hi[:, k, cols], start=k == 0, stop=False)
                mm(bank, wh, act_lo[:, k, cols], start=False, stop=False)
                ins = mm(bank, wl, act_hi[:, k, cols], start=False, stop=k == KT - 1)
                if k == KT - 1:
                    pj.pe_post(ins, key)

            def pairs(bank, h, lhsT, rhs, post, more=()):
                for c in range(8):
                    for hd in range(2):
                        r, col = slice(hd * HD, hd * HD + HD), slice((8 * h + c) * CH, (8 * h + c + 1) * CH)
                        terms = [(lhsT, rhs), *more]
                        for n, (a, b) in enumerate(terms):
                            ins = mm(bank[r, c * CH:(c + 1) * CH], a(r, col), b(r, col), start=n == 0,
                                     stop=n == len(terms) - 1)
                post(ins)

            def unit(ring, key):
                return ring.pe_open(pe, key), lambda ins: ring.pe_post(ins, key)

            def of(i):
                return lambda r, col: A[r, i, col]

            def lora_(p):
                pe.wait_ge(sem("consts_loaded"), 16 * N_CONSTS)
                pe.wait_ge(sem("xw_tanh"), 1)
                for w, r in (("z", slice(0, 32)), ("a", slice(32, 64))):
                    for h in range(2):
                        bank, post = unit(rw, (w, p, h))
                        post(mm(bank[:, :], lora_sb[r, p * P:(p + 1) * P], xm[r, hs(h)], start=True, stop=True))

            def block_sum(name, p, src, ready):
                for h in range(2):
                    ready(h)
                    bank, post = unit(rw, (name, p, h))
                    post(mm(bank[:, :], blk, src[:, hs(h)], start=True, stop=True))

            def kkn(p):
                block_sum("kkn", p, A[:, rP1, :], lambda h: pe.wait_ge(sem("kk_sq"), 2 * p + h + 1))

            def bon(p):
                block_sum("bon", p, A[:, rTT, :], lambda h: pe.wait_ge(sem("rk_ready"), p + 1))

            def tok(kind, p, h):
                src = {"v": A[:, rv], "b": A[:, ra], "k": A[:, rk], "hv": A[:, hatt], "hk": A[:, hk]}[kind]
                if kind == "v":
                    pe.wait_ge(sem("shift_done"), shift_no[("rw", p, "v")] + 1)
                elif kind in "bk":
                    pe.wait_ge(sem("bars_ready"), p + 1)
                elif kind == "hv":
                    pj.wait_read(pe, ("h", p, "i", h))
                else:
                    pe.wait_ge(sem("hk_ready"), p + 1)
                bank, post = unit(rw, ("tok", kind, p, h))
                pairs(bank, h, lambda r, col: src[r, col], lambda r, col: ident[r, r], post)

            def minit(p, h):
                pe.wait_ge(sem("bars_ready"), p + 1)
                bank, post = unit(rw, ("L", p, h))
                pairs(bank, h, of(rkk), of(ra), post)
                bank, post = unit(rw, ("M", p, h))
                pairs(bank, h, of(ra), of(rkk), post)

            def invp(p, l, h):
                if l == 1:
                    rw.wait_read(pe, ("M", p, h))
                else:
                    rw.wait_read(pe, ("dT", p, l - 1, h))
                bank, post = unit(rw, ("P1", p, l, h))
                pairs(bank, h, of(rL), of(rTT), post)

            def invt(p, l, h):
                rw.wait_read(pe, ("P1", p, l, h))
                bank, post = unit(rw, ("dTT", p, l, h))
                pairs(bank, h, of(rT), of(rP1), post)
                if l < 5:
                    bank, post = unit(rw, ("dT", p, l, h))
                    pairs(bank, h, of(rP1), of(rT), post)

            def mk3(w, p, h):
                a, b = {"ak": (rk, rkk), "rb": (ra, rr), "rk": (rk, rr)}[w]
                bank, post = unit(rw, (w, p, h))
                pairs(bank, h, of(a), of(b), post)

            def cr(p, c):
                col = slice(c * CH, (c + 1) * CH)
                if c == 0:
                    rw.wait_read(pe, ("rk", p, 1))
                    for kind in "vbk":
                        rw.wait_read(pe, ("tok", kind, p, 1))
                bank, post = unit(rw, ("R", p, c))
                if c:
                    rw.wait_read(pe, ("S", p, c - 1))
                for r in heads:
                    ins = mm(bank[r, 0:CH], A[r, rMak, col], A[r, rVt, col], start=True, stop=c == 0)
                    if c:
                        ins = mm(bank[r, 0:CH], A[r, rkk, col], S_st[r, c % 2, :], start=False, stop=True)
                post(ins)

            def cu(p, c):
                rw.wait_read(pe, ("R", p, c))
                bank, post = unit(rw, ("U", p, c))
                for r in heads:
                    ins = mm(bank[r, 0:CH], A[r, rTT, c * CH:(c + 1) * CH], R_sb[r, :], start=True, stop=True)
                post(ins)

            def cs(p, c):
                col = slice(c * CH, (c + 1) * CH)
                rw.wait_read(pe, ("U", p, c))
                if c < NC - 1:
                    bank, post = unit(rw, ("S", p, c))
                    for r in heads:
                        mm(bank[r, 0:CH], A[r, rKt, col], A[r, rVt, col], start=True, stop=False)
                        ins = mm(bank[r, 0:CH], A[r, rBt, col], U_sb[r, :], start=False, stop=True)
                    post(ins)
                bank, post = unit(rw, ("Y", p, c))
                for r in heads:
                    mm(bank[r, 0:CH], A[r, rVt, col], A[r, rMrk, col], start=True, stop=False)
                    ins = mm(bank[r, 0:CH], U_sb[r, :], A[r, rMrb, col], start=False, stop=c == 0)
                    if c:
                        ins = mm(bank[r, 0:CH], S_st[r, c % 2, :], A[r, rr, col], start=False, stop=True)
                post(ins)

            def mu(p):
                block_sum("mu", p, A[:, rkk, :], lambda h: rw.wait_read(pe, ("Y", p, 8 * h + 7)))

            def var(p):
                block_sum("var", p, A[:, rP1, :], lambda h: pe.wait_ge(sem("yc_sq"), 2 * p + h + 1))

            def cmean():
                pe.wait_ge(sem("conv_acc"), 1)
                for h in range(2):
                    bank, post = unit(rw, ("cmean", h))
                    mm(bank[:, :], negone, yT[:, 6, hs(h)], start=True, stop=False)
                    post(mm(bank[:, :], negone, yT[:, 7, hs(h)], start=False, stop=True))

            def cvar():
                for h in range(2):
                    pe.wait_ge(sem("conv_sq"), 2 * h + 2)
                    bank, post = unit(rw, ("cvar", h))
                    mm(bank[:, :], negone, yT[:, 4, hs(h)], start=True, stop=False)
                    post(mm(bank[:, :], negone, yT[:, 5, hs(h)], start=False, stop=True))

            def hdiag(p, h):
                pe.wait_ge(sem("hqk_ready"), p + 1)
                bank, post = unit(rw, ("hdiag", p, h))
                pairs(bank, h, of(hk), of(hq), post)

            def hlev(p, l, h):
                pe.wait_ge(sem("hz_ready"), 2 * (6 * p + l) + h + 1)
                bank, post = unit(rw, ("hlev", p, l, h))
                pairs(bank, h, of(hlev_buf(l)), of(hlev_buf(l)), post)

            def hkv(p, h):
                rw.wait_read(pe, ("tok", "hk", p, h))
                bank, post = unit(rw, ("hkv", p, h))
                pairs(bank, h, of(hKt), of(hVt), post)

            def hout(p, h):
                rw.wait_read(pe, ("hkv", p, h))
                bank, post = unit(rw, ("hout", p, h))
                pairs(bank, h, of(hVt), of(hatt), post, more=[(of(hz), of(hq))])

            def hvar(p):
                block_sum("hvar", p, A[:, hx, :], lambda h: pe.wait_ge(sem("ho_sq"), 2 * p + h + 1))

            def sv(p):
                for h in range(2):
                    pj.wait_read(pe, ("s", p, "v", h))
                for h in range(2):
                    bank = sz.pe_open(pe, ("sv", p, h))
                    for c in range(4):
                        ins = tr(bank[:, c * P:(c + 1) * P], B[:, 3, (4 * h + c) * P:(4 * h + c + 1) * P], ident)
                    sz.pe_post(ins, ("sv", p, h))

            def sbz(p, hd, th, u):
                if u == 0:
                    for h in range(2):
                        pj.wait_read(pe, ("s", p, "q", h))
                        pj.wait_read(pe, ("s", p, "k", h))
                        sz.wait_read(pe, ("sv", p, h))
                r = slice(hd * HD, hd * HD + HD)
                j = sb_blocks(th)[u]
                key = ("z", p, hd, th, j)
                bank = sz.pe_open(pe, key)
                a, n = sb_cols(th, j)
                sz.pe_post(mm(bank[:, a:a + n], B[r, 1, j * P:(j + 1) * P], B[r, 0, th * HALF + a:th * HALF + a + n],
                              start=True, stop=True), key)

            def sbt(p, hd, th, u):
                j = sb_blocks(th)[u]
                key = ("z", p, hd, th, j)
                bank = sz.bank(key)
                a, n = sb_cols(th, j)
                pe.wait_ge(sem("sp_ready"), sb_index(p, hd, th, j) + 1)
                spb = B[:, 4, (u % 2) * HALF:(u % 2) * HALF + HALF]
                ins = mm(bank[:, a:a + n], tri, spb[:, a:a + n], start=False, stop=u == 0, skip_group_check=True)
                if u:
                    rsb = B[:, 6, (u % 2) * HALF:(u % 2) * HALF + HALF]
                    a, n = sb_cols(th, j + 1)
                    ins = mm(bank[:, a:a + n], negone, rsb[:, a:a + n], start=False, stop=True, skip_group_check=True)
                sz.pe_post(ins, key)

            def sbv(p, hd, th, u):
                r = slice(hd * HD, hd * HD + HD)
                j = sb_blocks(th)[u]
                a, n = sb_cols(th, j)
                if u == 0:
                    so.pe_open(pe, ("o", p, hd, th))
                if j >= 4 * th:
                    pe.wait_ge(sem("at_ready"), sb_diag_index(p, hd, th, j) + 1)
                else:
                    sz.wait_read(pe, ("z", p, hd, th, j))
                bank = so.bank(("o", p, hd, th))
                atb = B[:, 5, (u % 2) * HALF:(u % 2) * HALF + HALF]
                ins = mm(bank[r, a:a + n], B[:, 2, j * P + hd * HD:j * P + hd * HD + HD], atb[:, a:a + n],
                         start=u == 0, stop=j == 0, skip_group_check=True)
                if j == 0:
                    so.pe_post(ins, ("o", p, hd, th))
                else:
                    ins.then_inc(sem("av_done"), 1)

            def vtr(n):
                pj.wait_read(pe, ("mv", n, 0))
                bank = pj.pe_open(pe, ("vtr", n))
                for mi in range(2):
                    ins = tr(bank[:, mi * P:(mi + 1) * P], kv_vt(n)[:, mi * P:(mi + 1) * P], ident)
                pj.pe_post(ins, ("vtr", n))

            def wide(name, n, i):
                m = wides.index((name, n))
                tok_ = slice(i * P, (i + 1) * P)
                if n == 0:
                    if name == "o":
                        pe.wait_ge(sem("y_split"), i + 1)
                    else:
                        av_ring.wait_read(pe, ("aval", i, 1))
                key = ("wide", name, n, i)
                bank = pj.pe_open(pe, key)[:, 0:256]
                for k in range(KT):
                    if i == 0 and k % 2 == 0:
                        pe.wait_ge(sem("v_split"), 4 * m + k // 2 + 1)
                    ah, al = act_hi[:, k, tok_], act_lo[:, k, tok_]
                    mm(bank, ah, vhi[:, (m + 1) % 2, k, :], start=k == 0, stop=False)
                    mm(bank, ah, wide_lo(m)[:, k, :], start=False, stop=False)
                    ins = mm(bank, al, vhi[:, (m + 1) % 2, k, :], start=False, stop=k == KT - 1)
                pj.pe_post(ins, key)

            def ascore(i, g):
                if (i, g) == (0, 0):
                    for h in range(2):
                        pj.wait_read(pe, ("q", KT - 1, h))
                key = ("ascore", i, g)
                bank = rw.pe_open(pe, key)
                for e in range(2):
                    for d in range(2):
                        n = 4 * g + 2 * e + d
                        ins = mm(bank[:, e * M:(e + 1) * M], yT[:, n, i * P:(i + 1) * P], kT_of(n), start=d == 0,
                                 stop=d == 1)
                rw.pe_post(ins, key)

            def aturn(i, g):
                key = ("aturn", i, g)
                pe.wait_ge(sem("p_ready"), 2 * i + g + 1)
                bank = sz.pe_open(pe, key)
                for b in range(4):
                    ins = tr(bank[:, b * P:(b + 1) * P], prob[g][:, b * P:(b + 1) * P], ident)
                sz.pe_post(ins, key)

            def aval(i, g):
                key = ("aval", i, g)
                sz.wait_read(pe, ("aturn", i, g))
                bank = av_ring.pe_open(pe, key)
                for e in range(2):
                    for d in range(2):
                        n = 4 * g + 2 * e + d
                        o = bank[:, (2 * e + d) * P:(2 * e + d + 1) * P]
                        for mi in range(2):
                            ins = mm(o, kv[:, 2 + mi, n * P:(n + 1) * P],
                                     probT[g][:, (2 * e + mi) * P:(2 * e + mi + 1) * P], start=mi == 0, stop=mi == 1)
                av_ring.pe_post(ins, key)

            run({"xT": xT, "mT": mT, "piece": piece, "lora": lora_, "kkn": kkn, "bon": bon, "tok": tok,
                 "minit": minit, "invp": invp, "invt": invt, "mk3": mk3, "cr": cr, "cu": cu, "cs": cs, "mu": mu,
                 "var": var, "cmean": cmean, "cvar": cvar, "hdiag": hdiag, "hlev": hlev, "hkv": hkv, "hout": hout,
                 "hvar": hvar, "sv": sv, "sbz": sbz, "sbt": sbt, "sbv": sbv,
                 "vtr": vtr, "hT": hT, "wide": wide, "ascore": ascore, "aturn": aturn, "aval": aval})

        @block.scalar
        def _(act):
            loaded = [None]

            def av(out, in_, func, **kw):
                want = {ACT.Exp: EXP_SET, ACT.Ln: EXP_SET, ACT.Sigmoid: SIG_SET, ACT.Tanh: SIG_SET}.get(func)
                if want and want != loaded[0]:
                    act.preload_act_table_set(want)
                    loaded[0] = want
                return nc.scalar.activation(out, in_, func, **kw)

            def derive():
                act.wait_ge(sem("lb_diff"), 1)
                done(act, av(d0("e", 0, 2), d0("e", 0, 2), ACT.Exp), "lb_exp")

            def exp(out, in_, name=None, scale=1.0, bias=0.0):
                done(act, av(out, in_, ACT.Exp, scale=scale, bias=bias), name or "act_step")

            def row_norm(src, junk, col):
                done(act, av(junk, src, ACT.Square, accum_out=stat[:, col:col + 1]), "act_step")
                done(act, av(stat[:, 32 + col:33 + col], stat[:, col:col + 1], ACT.Ln, scale=1.0 / D, bias=eps_ap(RMS_EPS)),
                     "act_step")
                exp(stat[:, 64 + col:65 + col], stat[:, 32 + col:33 + col], scale=-0.5, name="row_norm")

            def xn(i):
                if i == 0:
                    act.wait_ge(sem("eps_set"), 1)
                act.wait_ge(sem(f"x_loaded{i % 2}"), 16 * (i // 2 + 1))
                row_norm(A[:, i % 2, :], A[:, 5, :], i)

            def mn(i):
                act.wait_ge(sem("mem_loaded"), 48)
                row_norm(B[:, 4 + i, :], B[:, 2 + i, :], 8 + i)

            def hi_part(name, i):
                for q in range(2):
                    bank = pj.rd_open(act, (name, i, q))
                    pj.rd_done(act, nc.scalar.copy(act_hi[:, 4 * q:4 * q + 4, i * P:(i + 1) * P],
                                                   bank.rearrange("p (c t) -> p c t", c=4)), (name, i, q))

            def copy_out(ring, key, dst, scale=None, func=None, bias=None):
                bank = ring.rd_open(act, key)
                src = bank[:, 0:dst_cols(dst)]
                if func is not None:
                    ins = av(dst, src, func, bias=0.0 if bias is None else bias, scale=1.0 if scale is None else scale)
                elif scale is not None:
                    ins = nc.scalar.mul(dst, src, scale)
                else:
                    ins = nc.scalar.copy(dst, src)
                ring.rd_done(act, ins, key)

            def proj(*key):
                kind, h = key[:-1], key[-1]
                g, what = kind[0], kind[-1]
                if kind in shift_list:
                    if h == 0:
                        if shift_no[kind]:
                            act.wait_ge(sem("shift_done"), shift_no[kind])
                        else:
                            act.wait_ge(sem("pool_init"), 3)
                    copy_out(pj, key, raw[:, 1 + h * HALF:1 + (h + 1) * HALF])
                elif what == "gate":
                    y = gate_tile(kind)
                    if y >= 4:
                        act.wait_ge(sem("conv_done"), 2)
                    copy_out(pj, key, yT[:, y, hs(h)], func=ACT.Sigmoid)
                elif g == "cv" and what == "glu":
                    copy_out(pj, key, yT[:, 4 + kind[1], hs(h)], func=ACT.Sigmoid)
                elif g == "h":
                    if h == 0:
                        act.wait_ge(sem("rw_done"), 2)
                        if kind[1]:
                            act.wait_ge(sem("h_done"), kind[1])
                    if what == "q":
                        copy_out(pj, key, A[:, hq, hs(h)], func=ACT.Sigmoid)
                    elif what == "i":
                        copy_out(pj, key, A[:, hatt, hs(h)])
                    elif what == "f":
                        copy_out(pj, key, A[:, hz, hs(h)])
                        done(act, av(A[:, hx, hs(h)], A[:, hz, hs(h)], ACT.Sigmoid), "act_step")
                        done(act, av(A[:, hk, hs(h)], A[:, hz, hs(h)], ACT.Sigmoid, scale=-1.0), "hf_sig")
                elif g == "s":
                    if kind[1] and h == 0:
                        so.wait_read(act, ("o", 0, 1, 1))
                    if what == "q":
                        copy_out(pj, key, B[:, 0, hs(h)], scale=HD ** -0.5)
                    elif what == "k":
                        copy_out(pj, key, B[:, 1, hs(h)])
                    elif what == "v":
                        copy_out(pj, key, B[:, 3, hs(h)])
                elif g == "mk":
                    copy_out(pj, key, kT_of(kind[1]))
                elif g == "mv":
                    if kind[1] >= 2:
                        pj.rd_open(act, ("vtr", kind[1] - 2))
                    copy_out(pj, key, kv_vt(kind[1]))
                elif g == "q":
                    copy_out(pj, key, yT[:, kind[1], hs(h)], scale=float(D // 4) ** -0.5)

            def xwt():
                act.wait_ge(sem("derived"), 1)
                act.wait_ge(sem("shift_done"), shift_no[("xw",)] + 1)
                done(act, av(xm[0:32, :], xm[0:32, :], ACT.Tanh), "xw_tanh")

            def lora_(p):
                if p:
                    act.wait_ge(sem("rw_done"), p)
                for h in range(2):
                    copy_out(rw, ("z", p, h), A[:, rS, hs(h)], func=ACT.Sigmoid, bias=c0("w0", p))
                for h in range(2):
                    copy_out(rw, ("a", p, h), A[:, ra, hs(h)], func=ACT.Sigmoid, bias=c0("a0", p))

            def rwa(p):
                for h in range(2):
                    act.wait_ge(sem("kk_scaled"), p + 1)
                    done(act, av(A[:, rP1, hs(h)], A[:, rkk, hs(h)], ACT.Square), "kk_sq")
                act.wait_ge(sem("scan_done"), p + 1)
                exp(A[:, rBt, :], A[:, rC, :], scale=DECAY, name="e_incl")
                exp(A[:, rKt, :], A[:, rC, :], scale=-DECAY, name="e_neg")
                exp(DC[:, :], A[:, rC, CH - 1:T:CH], scale=DECAY, name="e_chunk")
                act.wait_ge(sem("s_excl"), p + 1)
                exp(A[:, rS, :], A[:, rS, :], scale=DECAY, name="e_excl")

            def kkn(p):
                for h in range(2):
                    rw.wait_read(act, ("kkn", p, h))
                    done(act, av(A[:, rP1, hs(h)], A[:, rP1, hs(h)], ACT.Ln, scale=KK_SCALE), "act_step")
                    exp(A[:, rP1, hs(h)], A[:, rP1, hs(h)], scale=-0.5, name="kk_inv")

            def tok(kind, p, h):
                dst = {"v": rVt, "b": rBt, "k": rKt, "hv": hVt, "hk": hKt}[kind]
                copy_out(rw, ("tok", kind, p, h), A[:, dst, hs(h)])

            def minit(p, h):
                copy_out(rw, ("L", p, h), A[:, rL, hs(h)])

            def invp(p, l, h):
                bank = rw.rd_open(act, ("P1", p, l, h))
                rw.rd_done(act, nc.scalar.copy(level_half(A[:, rP1, hs(h)], l, 1), level_half(bank, l, 1)),
                           ("P1", p, l, h))

            def cr(p, c):
                copy_out(rw, ("R", p, c), R_sb[:, :])

            def cu(p, c):
                copy_out(rw, ("U", p, c), U_sb[:, :])

            def cs(p, c):
                copy_out(rw, ("Y", p, c), A[:, rkk, c * CH:(c + 1) * CH])

            def mu(p):
                for h in range(2):
                    rw.wait_read(act, ("mu", p, h))
                    done(act, av(A[:, rP1, hs(h)], A[:, rkk, hs(h)], ACT.Square), "yc_sq")

            def var(p):
                for h in range(2):
                    copy_out(rw, ("var", p, h), A[:, rTT, hs(h)], func=ACT.Ln, scale=1.0 / HD, bias=eps_ap(RWKV_EPS))
                    exp(A[:, rTT, hs(h)], A[:, rTT, hs(h)], scale=-0.5, name="y_rs")

            def csq():
                for h in range(2):
                    rw.wait_read(act, ("cmean", h))
                    for i in range(2):
                        done(act, av(yT[:, 4 + i, hs(h)], yT[:, 6 + i, hs(h)], ACT.Square), "conv_sq")

            def cvar():
                for h in range(2):
                    copy_out(rw, ("cvar", h), yT[:, 4, hs(h)], func=ACT.Ln, scale=-1.0 / G, bias=eps_ap(LN_EPS))
                    exp(yT[:, 4, hs(h)], yT[:, 4, hs(h)], scale=-0.5, name="conv_rs")

            def cfin():
                for i in range(2):
                    act.wait_ge(sem("conv_y"), i + 1)
                    done(act, av(yT[:, 5, :], yT[:, 6 + i, :], ACT.Sigmoid), "conv_sg")

            def hgate(p):
                act.wait_ge(sem("hf_floor"), p + 1)
                done(act, av(A[:, hx, :], A[:, hx, :], ACT.Ln, scale=d0("omlb", p), bias=d0("lb", p)), "hf_ln")

            def hlev(p, l, h):
                buf = A[:, hlev_buf(l), hs(h)].rearrange("p (b s w) -> p b s w", s=2, w=1 << l)
                act.wait_ge(sem("hdiff"), 2 * (6 * p + l) + h + 1)
                exp(buf[:, :, 0, :], buf[:, :, 0, :], scale=-1.0)
                exp(buf[:, :, 1, :], buf[:, :, 1, :], name="hexp")

            def hbars(p):
                rw.rd_open(act, ("hlev", p, 5, 1))
                exp(A[:, hz, :], A[:, hb, :], name="hq_exp")
                act.wait_ge(sem("hk_diff"), p + 1)
                exp(A[:, hx, :], A[:, hx, :], name="hk_exp")
                exp(DC[:, :], A[:, hb, CH - 1:T:CH], name="hdc")

            def hout(p, h):
                rw.wait_read(act, ("hout", p, h))
                done(act, av(A[:, hx, hs(h)], A[:, hk, hs(h)], ACT.Square), "ho_sq")

            def hvar(p):
                for h in range(2):
                    copy_out(rw, ("hvar", p, h), A[:, hb, hs(h)], func=ACT.Ln, scale=1.0 / HD, bias=eps_ap(RMS_EPS))
                    exp(A[:, hb, hs(h)], A[:, hb, hs(h)], scale=-0.5, name="ho_rs")

            def sv(p):
                for h in range(2):
                    copy_out(sz, ("sv", p, h), B[:, 2, hs(h)])

            def sbz(p, hd, th, u):
                j = sb_blocks(th)[u]
                key = ("z", p, hd, th, j)
                unit_no = sb_index(p, hd, th, j)
                bank = sz.rd_open(act, key)
                a, n = sb_cols(th, j)
                e = B[:, 3, (u % 2) * HALF + a:(u % 2) * HALF + a + n]
                if unit_no >= 2:
                    act.wait_ge(sem("sp_ready"), unit_no - 1)
                if u < 2:
                    for h in range(2):
                        sz.wait_read(act, ("sv", p, h))
                done(act, av(e, bank[:, a:a + n], ACT.Abs), "act_step")
                exp(e, e, scale=-1.0)
                done(act, av(e, e, ACT.Ln, bias=1.0), "sp_ln")

            def sbt(p, hd, th, u):
                j = sb_blocks(th)[u]
                key = ("z", p, hd, th, j)
                a, n = sb_cols(th, j)
                at = B[:, 5, (u % 2) * HALF:(u % 2) * HALF + HALF]
                bank = sz.bank(key)
                if j >= 4 * th:
                    sz.wait_read(act, key, nth=1)
                    if n > P:
                        sz.rd_done(act, av(at[:, a + P:a + n], bank[:, a + P:a + n], ACT.Exp), key, nth=2)
                    exp(at[:, a:a + P], at[:, a:a + P], name="at_ready")
                else:
                    sz.rd_open(act, key, post=2)
                    wait_av(act, sb_index(p, hd, th, j) - 2)
                    sz.rd_done(act, av(at[:, a:a + n], bank[:, a:a + n], ACT.Exp), key)

            def vtr(n):
                bank = pj.rd_open(act, ("vtr", n))
                pj.rd_done(act, nc.scalar.copy(v_of(n), bank[:, 0:M].rearrange("p (m v) -> p m v", m=2)), ("vtr", n))

            def ysplit(i):
                if i == 0:
                    mixers_done(act)
                    pj.rd_open(act, ("mv", KT - 1, 0))
                tok_ = slice(i * P, (i + 1) * P)
                done(act, nc.scalar.copy(act_hi[:, :, tok_], yT[:, :, tok_]), "y_hi")

            def x2n(i):
                if i == 0:
                    act.wait_ge(sem("y_split"), TT)
                pj.wait_read(act, ("wide", "o", 3, i))
                row_norm(x2[:, i, :], yT[:, 5, :], 10 + i)

            def fin(i):
                pj.wait_read(act, ("wide", "f", 3, i))
                row_norm(x2[:, i, :], yT[:, 2, :], 18 + i)

            def ascore(i, g):
                key = ("ascore", i, g)
                st_ = amax[g]
                rw.wait_read(act, key, nth=1)
                act.wait_ge(sem("a_max"), 2 * i + g + 1)
                for e in range(2):
                    src, dst = rw.bank(key)[:, e * M:(e + 1) * M], prob[g][:, e * M:(e + 1) * M]
                    ins = av(dst, src, ACT.Exp, bias=st_[:, e:e + 1], accum_out=st_[:, 2 + e:3 + e])
                    if e == 0:
                        done(act, ins, "act_step")
                    else:
                        rw.rd_done(act, ins, key, nth=2)

            def aturn(i, g):
                copy_out(sz, ("aturn", i, g), probT[g])

            def aval(i, g):
                key = ("aval", i, g)
                bank = av_ring.rd_open(act, key)
                av_ring.rd_done(act, nc.scalar.copy(act_hi[:, 4 * g:4 * g + 4, i * P:(i + 1) * P],
                                                    bank.rearrange("p (c t) -> p c t", c=4)), key)

            run({"derive": derive, "xn": xn, "mn": mn, "xT": lambda i: hi_part("xT", i), "mT": lambda i: hi_part("mT", i), "proj": proj,
                 "xwt": xwt, "lora": lora_, "rwa": rwa, "kkn": kkn, "tok": tok, "minit": minit, "invp": invp, "cr": cr,
                 "cu": cu, "cs": cs,
                 "mu": mu, "var": var, "csq": csq, "cvar": cvar, "cfin": cfin, "hgate": hgate, "hlev": hlev,
                 "hbars": hbars, "hout": hout, "hvar": hvar, "sv": sv, "sbz": sbz, "sbt": sbt, "vtr": vtr,
                 "ysplit": ysplit, "x2n": x2n, "hT": lambda i: hi_part("hT", i), "ascore": ascore, "aturn": aturn,
                 "aval": aval, "fin": fin})

        @block.vector
        def _(dve):
            V = nc.vector

            def ok(ins, name="dve_step"):
                done(dve, ins, name)

            def tt(out, a, b, op, name="dve_step"):
                ok(V.tensor_tensor(out, a, b, op), name)

            def stt(out, a, s, b, op0, op1, name="dve_step"):
                ok(V.scalar_tensor_tensor(out=out, in0=a, scalar=s, in1=b, op0=op0, op1=op1), name)

            def ts(out, a, s1, s2, op0, op1=None, name="dve_step"):
                ok(V.tensor_scalar(out, a, s1, s2, op0, op1) if op1 is not None
                   else V.tensor_scalar(out, a, s1, None, op0), name)

            ADD, SUB, MUL, MAX, MIN = ALU.add, ALU.subtract, ALU.mult, ALU.max, ALU.min

            for n_, e_ in enumerate(EPS):
                ok(V.memset(der[:, DER["eps"] + n_:DER["eps"] + n_ + 1], e_),
                   "eps_set" if n_ == len(EPS) - 1 else "dve_step")

            def derive():
                dve.wait_ge(sem("consts_loaded"), 16 * N_CONSTS)
                ok(V.tensor_copy(mcst[:], A[:, 6, 0:13 * CH]))
                ts(d0("omu", 0, 6), c0("mu", 0, 6), -1.0, 1.0, MUL, ADD)
                ts(d0("omux"), c0("mux"), -1.0, 1.0, MUL, ADD)
                ts(d0("oka", 0, 2), c0("k_a", 0, 2), -1.0, 1.0, MUL, ADD)
                tt(d0("e", 0, 2), c0("lbl", 0, 2), c0("lbl", 0, 2), SUB, "lb_diff")
                dve.wait_ge(sem("lb_exp"), 1)
                ok(V.reciprocal(d0("soft", 0, 2), d0("e", 0, 2)))
                tt(d0("soft", 0, 2), d0("soft", 0, 2), d0("e", 0, 2), MUL)
                tt(d0("lb", 0, 2), d0("soft", 0, 2), d0("soft", 0, 2), SUB)
                ts(d0("omlb", 0, 2), d0("lb", 0, 2), -1.0, 1.0, MUL, ADD, name="derived")

            def xn(i):
                if i == 0:
                    dve.wait_ge(sem("mix_gain_loaded"), 16)
                dve.wait_ge(sem("row_norm"), i + 1)
                if i >= 2:
                    pj.rd_open(dve, ("xT", i - 2, 1))
                stt(A[:, 2 + i % 2, :], A[:, i % 2, :], stat[:, 64 + i:65 + i], A[:, 4, :], MUL, MUL, "x_scaled")

            def mn(i):
                dve.wait_ge(sem("row_norm"), TT + i + 1)
                stt(B[:, 4 + i, :], B[:, 4 + i, :], stat[:, 72 + i:73 + i], B[:, 6, :], MUL, MUL, "m_scaled")

            def lo_part(name, i):
                for q in range(2):
                    key = (name, i, q)
                    pj.wait_read(dve, key, nth=1)
                    dst = (slice(None), slice(4 * q, 4 * q + 4), slice(i * P, (i + 1) * P))
                    pj.rd_done(dve, V.tensor_tensor(act_lo[dst], pj.bank(key).rearrange("p (c t) -> p c t", c=4),
                                                    act_hi[dst].bitcast(F32), SUB), key, nth=2)

            def proj(*key):
                kind, h = key[:-1], key[-1]
                g, what = kind[0], kind[-1]
                if kind in shift_list:
                    if h == 0:
                        return
                    if g == "xw":
                        dst, mu_, omu_, r = xm[:, :], c0("mux"), d0("omux"), slice(0, 64)
                    else:
                        n = "rkv".index(what) * 2 + kind[1]
                        dst, mu_, omu_, r = A[:, {"r": rr, "k": rk, "v": rv}[what], :], c0("mu", n), d0("omu", n), \
                            slice(0, P)
                    for q in range(2):
                        pj.wait_read(dve, kind + (q,))
                    ts(dst, raw[r, 1:1 + T], omu_[r, :], None, MUL)
                    stt(dst, raw[r, 0:T], mu_[r, :], dst, MUL, ADD, "shift_done")
                elif what == "gate" or (g, what) == ("h", "q"):
                    dst = yT[:, gate_tile(kind), hs(h)] if what == "gate" else A[:, hq, hs(h)]
                    pj.wait_read(dve, key, nth=1)
                    pj.rd_done(dve, V.tensor_tensor(dst, dst, pj.bank(key), MUL), key, nth=2)
                elif g == "cv" and what == "val":
                    pj.wait_read(dve, ("cv", kind[1], "glu", h))
                    u = yT[:, 4 + kind[1], hs(h)]
                    pj.rd_done(dve, V.tensor_tensor(u, u, pj.rd_open(dve, key), MUL), key)

            def conv(i, s):
                w = c0("cw", i * CW + CW - 1 - s)
                u, acc = yT[:, 4 + i, 0:T - s], yT[:, 6 + i, s:T]
                if s == 0:
                    ts(acc, u, w, c0("cb", i), MUL, ADD)
                else:
                    stt(acc, u, w, acc, MUL, ADD, "conv_acc" if (i, s) == (1, CW - 1) else "dve_step")

            def cmean():
                for h in range(2):
                    bank = rw.rd_open(dve, ("cmean", h))
                    for i in range(2):
                        acc = yT[:, 6 + i, hs(h)]
                        rw.rd_done(dve, V.scalar_tensor_tensor(out=acc, in0=bank, scalar=1.0 / G, in1=acc, op0=MUL,
                                                               op1=ADD), ("cmean", h), nth=i + 1)

            def cfin():
                for i in range(2):
                    acc = yT[:, 6 + i, :]
                    if i == 0:
                        dve.wait_ge(sem("conv_rs"), 2)
                    stt(acc, acc, c0("cln_g", i), yT[:, 4, :], MUL, MUL)
                    ts(acc, acc, c0("cln_b", i), None, ADD, name="conv_y")
                    dve.wait_ge(sem("conv_sg"), i + 1)
                    tt(acc, acc, yT[:, 5, :], MUL)
                    tt(yT[:, 2 + i, :], yT[:, 2 + i, :], acc, MUL, "conv_done")

            def rwa(p):
                for h in range(2):
                    rw.wait_read(dve, ("z", p, h))
                    rw.wait_read(dve, ("a", p, h))
                ok(V.tensor_tensor_scan(A[:, rC, :], reset[:, :], A[:, rS, :], 0.0, MUL, ADD), "scan_done")
                tt(A[:, rS, :], A[:, rC, :], A[:, rS, :], SUB, "s_excl")
                ts(A[:, rkk, :], A[:, rk, :], c0("k_k", p), None, MUL, name="kk_scaled")
                ts(A[:, rTT, :], A[:, ra, :], c0("k_a", p), d0("oka", p), MUL, ADD)
                tt(A[:, rk, :], A[:, rk, :], A[:, rTT, :], MUL)
                stt(A[:, rTT, :], A[:, rr, :], c0("r_k", p), A[:, rk, :], MUL, MUL, "rk_ready")
                dve.wait_ge(sem("e_incl"), p + 1)
                tt(A[:, rr, :], A[:, rr, :], A[:, rBt, :], MUL)

            def kkn(p):
                for h in range(2):
                    bank = rw.rd_open(dve, ("kkn", p, h))
                    rw.rd_done(dve, V.tensor_scalar(A[:, rP1, hs(h)], bank, 1e-24, None, MAX), ("kkn", p, h))

            def rwb(p):
                for h in range(2):
                    dve.wait_ge(sem("kk_inv"), 2 * p + h + 1)
                    stt(A[:, rkk, hs(h)], A[:, rP1, hs(h)], KK_SCALE ** 0.5, A[:, rkk, hs(h)], MUL, MUL)
                tt(A[:, ra, :], A[:, ra, :], A[:, rkk, :], MUL)
                dve.wait_ge(sem("e_neg"), p + 1)
                tt(A[:, ra, :], A[:, ra, :], A[:, rKt, :], MUL)
                tt(A[:, rk, :], A[:, rk, :], A[:, rKt, :], MUL)
                dve.wait_ge(sem("e_excl"), p + 1)
                stt(A[:, rkk, :], A[:, rkk, :], -1.0, A[:, rS, :], MUL, MUL, "bars_ready")

            def bon(p):
                rw.rd_open(dve, ("tok", "v", p, 1))
                for h in range(2):
                    bank = rw.rd_open(dve, ("bon", p, h))
                    rw.rd_done(dve, V.tensor_tensor(A[:, rv, hs(h)], A[:, rv, hs(h)], bank, MUL), ("bon", p, h))

            def chunks(ap):
                return ap.rearrange("p (c t) -> p c t", t=CH)

            def level_copy(dst, mask, src, l, bit):
                v = lambda ap: ap.rearrange("p (c b s w) -> p c b s w", s=2, w=1 << l, b=CH >> (l + 1))[:, :, :, bit, :]
                n = dst.shape[1] // CH
                shape = [P, n, CH >> (l + 1), 1 << l]
                return V.copy_predicated(v(dst), level_half(mask, l, bit).unsqueeze(1).broadcast_to(shape), v(src))

            def masked_copy(dst, mask, src):
                n = dst.shape[1] // CH
                return V.copy_predicated(chunks(dst), mask.unsqueeze(1).broadcast_to([P, n, CH]), chunks(src))

            def minit(p, h):
                eye = mcst[:, 12 * CH:13 * CH].unsqueeze(1).broadcast_to([P, NC // 2, CH])
                ok(V.tensor_copy(cm(A[:, rTT, hs(h)]), eye))
                dve.wait_ge(sem("e_excl"), p + 1)
                ok(V.tensor_copy(cm(A[:, rT, hs(h)]), eye))
                rw.wait_read(dve, ("L", p, h), nth=1)
                rw.rd_done(dve, masked_copy(A[:, rT, hs(h)], lev(6), rw.bank(("L", p, h))), ("L", p, h), nth=2)
                bank = rw.rd_open(dve, ("M", p, h))
                rw.rd_done(dve, masked_copy(A[:, rTT, hs(h)], lev(0), bank), ("M", p, h))

            def invt(p, l, h):
                for w, dst, m, bit in (("dTT", rTT, l, 1), ("dT", rT, 6 + l, 0))[:2 if l < 5 else 1]:
                    bank = rw.rd_open(dve, (w, p, l, h))
                    rw.rd_done(dve, level_copy(A[:, dst, hs(h)], lev(m), bank, l, bit), (w, p, l, h))

            def mk3(w, p, h):
                dst, m = {"ak": (rMak, m_strict), "rb": (rMrb, m_incl), "rk": (rMrk, m_incl)}[w]
                bank = rw.rd_open(dve, (w, p, h))
                rw.rd_done(dve, V.tensor_tensor(chunks(A[:, dst, hs(h)]), chunks(bank[:, :]),
                                                m.unsqueeze(1).broadcast_to([P, 8, CH]), MUL), (w, p, h))

            def cs(p, c):
                if c == NC - 1:
                    return
                s_new, scaled = S_st[:, (c + 1) % 2, :], S_dec[:, :]
                if c == 0:
                    dve.wait_ge(sem("e_chunk"), p + 1)
                bank = rw.rd_open(dve, ("S", p, c))[:, 0:CH]
                dc = DC[:, c:c + 1]
                if c == 0:
                    ins = V.tensor_scalar(s_new, bank, dc, None, MUL)
                else:
                    ins = V.scalar_tensor_tensor(out=s_new, in0=bank, scalar=dc, in1=scaled, op0=MUL, op1=ADD)
                rw.rd_done(dve, ins, ("S", p, c))
                if c < NC - 2:
                    ts(scaled, s_new, DC[:, c + 1:c + 2], None, MUL)

            def mu(p):
                for h in range(2):
                    bank = rw.rd_open(dve, ("mu", p, h))
                    y = A[:, rkk, hs(h)]
                    rw.rd_done(dve, V.scalar_tensor_tensor(out=y, in0=bank, scalar=-1.0 / HD, in1=y, op0=MUL,
                                                           op1=ADD), ("mu", p, h))

            def rfin(p):
                dve.wait_ge(sem("y_rs"), 2 * p + 2)
                y = A[:, rkk, :]
                stt(y, y, c0("rln_g", p), A[:, rTT, :], MUL, MUL)
                stt(y, y, c0("rln_b", p), A[:, rv, :], ADD, ADD)
                tt(yT[:, p, :], yT[:, p, :], y, MUL, "rw_done")

            def hgate(p):
                dve.wait_ge(sem("hf_sig"), 2 * p + 2)
                ts(A[:, hx, :], A[:, hx, :], LN_FLOOR, None, MAX, name="hf_floor")
                ts(A[:, hk, :], A[:, hk, :], d0("omlb", p), None, MUL, name="hqk_ready")
                dve.wait_ge(sem("hf_ln"), p + 1)
                tt(A[:, hx, :], A[:, hx, :], A[:, hz, :], MIN)
                ok(V.tensor_tensor_scan(A[:, hb, :], reset[:, :], A[:, hx, :], 0.0, MUL, ADD))
                for h in range(2):
                    hdiff(p, 0, h)

            def hdiff(p, l, h):
                w = 1 << l
                b = A[:, hb, hs(h)].rearrange("p (b w) -> p b w", w=2 * w)
                o = A[:, hlev_buf(l), hs(h)].rearrange("p (b w) -> p b w", w=2 * w)
                tt(o, b, b[:, :, w - 1:w].broadcast_to([P, HALF // (2 * w), 2 * w]), SUB, "hdiff")

            def hdiag(p, h):
                rw.rd_open(dve, ("tok", "hv", p, h))
                ok(V.memset(A[:, hatt, hs(h)], 0.0))
                bank = rw.rd_open(dve, ("hdiag", p, h))
                rw.rd_done(dve, masked_copy(A[:, hatt, hs(h)], lev(12), bank), ("hdiag", p, h))

            def hlev_out(p, l, h):
                bank = rw.rd_open(dve, ("hlev", p, l, h))
                rw.rd_done(dve, level_copy(A[:, hatt, hs(h)], lev(l), bank, l, 1), ("hlev", p, l, h))

            def hlev(p, l, h):
                v = lambda i: A[:, i, hs(h)].rearrange("p (b s w) -> p b s w", s=2, w=1 << l)
                buf = v(hlev_buf(l))
                dve.wait_ge(sem("hexp"), 2 * (6 * p + l) + h + 1)
                tt(buf[:, :, 0, :], buf[:, :, 0, :], v(hk)[:, :, 0, :], MUL)
                tt(buf[:, :, 1, :], buf[:, :, 1, :], v(hq)[:, :, 1, :], MUL, "hz_ready")
                if l:
                    hlev_out(p, l - 1, h)
                if l < 5:
                    hdiff(p, l + 1, h)

            def hbars(p):
                for h in range(2):
                    hlev_out(p, 5, h)
                tt(cm(A[:, hx, :]), cm(A[:, hb, :])[:, :, CH - 1:CH].broadcast_to([P, NC, CH]), cm(A[:, hb, :]), SUB,
                   "hk_diff")
                dve.wait_ge(sem("hq_exp"), p + 1)
                tt(A[:, hq, :], A[:, hq, :], A[:, hz, :], MUL)
                dve.wait_ge(sem("hk_exp"), p + 1)
                tt(A[:, hk, :], A[:, hk, :], A[:, hx, :], MUL, "hk_ready")

            def hkv(p, h):
                s = cm(A[:, hz, :])
                if h == 0:
                    ok(V.memset(s[:, 0, :], 0.0))
                    dve.wait_ge(sem("hdc"), p + 1)
                key, last = ("hkv", p, h), (7, NC - 2)[h]
                bank = rw.rd_open(dve, key)
                for c in range(8 * h, last + 1):
                    ins = V.scalar_tensor_tensor(out=s[:, c + 1, :], in0=s[:, c, :], scalar=DC[:, c:c + 1],
                                                 in1=bank[:, (c % 8) * CH:(c % 8 + 1) * CH], op0=MUL, op1=ADD)
                    if c == last:
                        rw.rd_done(dve, ins, key)
                    else:
                        ok(ins)

            def hout(p, h):
                bank = rw.rd_open(dve, ("hout", p, h))
                rw.rd_done(dve, V.tensor_copy(A[:, hk, hs(h)], bank), ("hout", p, h))

            def hfin(p):
                dve.wait_ge(sem("ho_rs"), 2 * p + 2)
                stt(A[:, hk, :], A[:, hk, :], c0("hn_g", p), A[:, hb, :], MUL, MUL)
                tt(yT[:, 4 + p, :], yT[:, 4 + p, :], A[:, hk, :], MUL, "h_done")

            def sbz(p, hd, th, u):
                blocks = sb_blocks(th)
                j = blocks[u]
                key = ("z", p, hd, th, j)
                first = sb_index(p, hd, th, blocks[0])
                bank = sz.bank(key)
                a, n = sb_cols(th, j)
                o = (u % 2) * HALF
                if u >= 2:
                    sz.rd_open(dve, ("z", p, hd, th, blocks[u - 2]), post=2)
                elif first:
                    so.rd_open(dve, so_before(p, hd, th))
                if u:
                    q = ((u - 1) % 2) * HALF
                    a1, n1 = sb_cols(th, blocks[u - 1])
                    a2, n2 = sb_cols(th, blocks[u - 2]) if u > 1 else (a1 + n1, 0)
                    if n2:
                        tt(B[:, 6, o + a2:o + a2 + n2], B[:, 6, q + a2:q + a2 + n2], B[:, 4, q + a2:q + a2 + n2], ADD)
                    if a2 > a1:
                        ok(V.tensor_copy(B[:, 6, o + a1:o + a2], B[:, 4, q + a1:q + a2]))
                dve.wait_ge(sem("sp_ln"), first + u + 1)
                diag = j >= 4 * th
                stt(B[:, 4, o + a:o + a + n], bank[:, a:a + n], 0.0, B[:, 3, o + a:o + a + n], MAX, ADD,
                    "dve_step" if diag else "sp_ready")
                if diag:
                    stt(B[:, 4, o + a:o + a + P], tri, 1.0, B[:, 4, o + a:o + a + P], ADD, MUL, "sp_ready")

            def sbt(p, hd, th, u):
                j = sb_blocks(th)[u]
                if j < 4 * th:
                    return
                key = ("z", p, hd, th, j)
                a, n = sb_cols(th, j)
                o = (u % 2) * HALF
                bank = sz.rd_open(dve, key, post=2)
                wait_av(dve, sb_index(p, hd, th, j) - 2)
                sz.rd_done(dve, V.scalar_tensor_tensor(out=B[:, 5, o + a:o + a + P], in0=tri, scalar=1e30,
                                                       in1=bank[:, a:a + P], op0=MUL, op1=ADD), key, nth=1)

            def sbo(p, hd, th):
                key = ("o", p, hd, th)
                bank = so.rd_open(dve, key)
                r = slice(hd * HD, hd * HD + HD)
                so.rd_done(dve, V.tensor_tensor(yT[r, 6 + p, hs(th)], yT[r, 6 + p, hs(th)], bank[r, :], MUL), key)

            def ysplit(i):
                dve.wait_ge(sem("y_hi"), i + 1)
                tok_ = slice(i * P, (i + 1) * P)
                tt(act_lo[:, :, tok_], yT[:, :, tok_], act_hi[:, :, tok_].bitcast(F32), SUB, "y_split")

            def wide(name, n, i):
                key = ("wide", name, n, i)
                if (name, n) == ("o", 0):
                    dve.wait_ge(sem(f"x2_loaded{i}"), 16)
                bank = pj.rd_open(dve, key)
                dst = x2[:, i, n * 256:(n + 1) * 256]
                pj.rd_done(dve, V.tensor_tensor(dst, dst, bank[:, 0:256], ADD), key)

            def x2n(i):
                if i == 0:
                    dve.wait_ge(sem("gain_loaded"), 16)
                dve.wait_ge(sem("row_norm"), TT + 2 + i + 1)
                if i >= 2:
                    pj.rd_open(dve, ("hT", i - 2, 1))
                stt(yT[:, 6 + i % 2, :], x2[:, i, :], stat[:, 74 + i:75 + i], yT[:, 4, :], MUL, MUL, "h_scaled")

            def fin(i):
                if i == 0:
                    dve.wait_ge(sem("gain_loaded"), 32)
                dve.wait_ge(sem("row_norm"), 2 * TT + 2 + i + 1)
                if i >= 2:
                    dve.wait_ge(sem(f"out_stored{i % 2}"), 16 * (i // 2))
                stt(yT[:, i % 2, :], x2[:, i, :], stat[:, 82 + i:83 + i], yT[:, 3, :], MUL, MUL, "out_ready")

            def ascore(i, g):
                key = ("ascore", i, g)
                st_ = amax[g]
                if i:
                    sz.rd_open(dve, ("aturn", i - 1, g))
                bank = rw.rd_open(dve, key)
                rw.rd_done(dve, V.tensor_reduce(st_[:, 4:6], bank.rearrange("p (e m) -> p e m", e=2), AX.X, MAX), key,
                           nth=1)
                ts(st_[:, 0:2], st_[:, 4:6], -1.0, None, MUL, name="a_max")
                rw.wait_read(dve, key)
                ok(V.reciprocal(st_[:, 6:8], st_[:, 2:4]))
                for e in range(2):
                    pe_ = prob[g][:, e * M:(e + 1) * M]
                    ts(pe_, pe_, st_[:, 6 + e:7 + e], None, MUL, name="p_ready" if e else "dve_step")

            def aval(i, g):
                key = ("aval", i, g)
                av_ring.wait_read(dve, key, nth=1)
                dst = (slice(None), slice(4 * g, 4 * g + 4), slice(i * P, (i + 1) * P))
                av_ring.rd_done(dve, V.tensor_tensor(act_lo[dst], av_ring.bank(key).rearrange("p (c t) -> p c t", c=4),
                                                     act_hi[dst].bitcast(F32), SUB), key, nth=2)

            run({"derive": derive, "xn": xn, "mn": mn, "xT": lambda i: lo_part("xT", i), "mT": lambda i: lo_part("mT", i), "proj": proj,
                 "conv": conv, "cmean": cmean, "cfin": cfin, "rwa": rwa, "rwb": rwb, "bon": bon, "minit": minit,
                 "kkn": kkn, "invt": invt, "mk3": mk3, "cs": cs, "mu": mu, "rfin": rfin, "hgate": hgate, "hdiag": hdiag,
                 "hlev": hlev, "hbars": hbars, "hkv": hkv, "hout": hout, "hfin": hfin, "sbz": sbz, "sbt": sbt, "sbo": sbo,
                 "ysplit": ysplit, "wide": wide, "x2n": x2n, "hT": lambda i: lo_part("hT", i), "ascore": ascore,
                 "aval": aval, "fin": fin})


_OUT = ((1, T, D), "float32")


def kernel(**inputs):
    import concourse.bacc as bacc
    from concourse import bass_utils

    v = {k: np.asarray(a) for k, a in inputs.items()}
    g2 = lambda a: a.reshape(-1, P).T
    chan = np.zeros((P, N_CHAN), np.float32)
    chan[:, CHAN["mu"]:CHAN["mu"] + 6] = g2(v["rwkv_mu"][0, :768])
    chan[:64, CHAN["mux"]] = v["rwkv_mu"][0, 768:]
    for name, src in (("w0", "rwkv_w0"), ("a0", "rwkv_a0"), ("k_k", "rwkv_k_k"), ("k_a", "rwkv_k_a"),
                      ("r_k", "rwkv_r_k"), ("rln_g", "rwkv_ln_g"), ("rln_b", "rwkv_ln_b"), ("cb", "conv_b"),
                      ("cln_g", "conv_ln_g"), ("cln_b", "conv_ln_b"), ("hn_g", "hgrn_norm_g"),
                      ("lbl", "hgrn_lb_logits")):
        chan[:, CHAN[name]:CHAN[name] + 2] = g2(v[src][0].reshape(G))
    chan[:, CHAN["cw"]:CHAN["cw"] + 2 * CW] = v["conv_w"][0].T.reshape(2, P, CW).transpose(1, 0, 2).reshape(P, 2 * CW)
    fconst, mconst = shape_constants()
    arrays = {
        "x": v["x"][0], "mem": v["mem"][0], "w_in": v["w_in"][0], "w_out": v["w_out"][0], "wq": v["xattn_wq"][0],
        "wk": v["xattn_wk"][0], "wv": v["xattn_wv"][0], "wo": v["xattn_wo"][0],
        "lora": np.concatenate([v["rwkv_w_up"][0], v["rwkv_a_up"][0]]),
        "chan": chan,
        "norms": np.stack([v["norm_mix"][0], v["norm_xattn"][0], v["norm_mem"][0], v["norm_final"]]),
        "fconst": fconst, "mconst": mconst,
    }
    nc = bacc.Bacc("TRN2", target_bir_lowering=False, num_devices=1)
    arrays = {f"in_{k}": np.ascontiguousarray(a) for k, a in arrays.items()}
    args = [nc.dram_tensor(k, a.shape, mybir.dt.from_np(a.dtype), kind="ExternalInput").ap()
            for k, a in arrays.items()]
    args.append(nc.dram_tensor("out_0", (T, D), F32, kind="ExternalOutput").ap())
    program(nc, *args)
    r = bass_utils.run_bass_kernel_spmd(nc, [arrays], core_ids=[0])
    return r.results[0]["out_0"].reshape(_OUT[0])
```
